# Optimizing a Trainium2 kernel written in Bass

```python
import math
import jax, jax.numpy as jnp
from jax import lax
import numpy as np

D_MODEL = 1024
BATCH = 1
SEQ = 512
DEPTH = 2

N_MIXERS = 2
N_Q_HEADS = 16
N_KV_HEADS = 2
HEAD_DIM = 64
QKV_DIM = (N_Q_HEADS + 2 * N_KV_HEADS) * HEAD_DIM
WINDOW = 128
ATTN_BLOCK = 128
N_REL_BUCKETS = 32
REL_MAX_DISTANCE = 128
CONV_DIM = D_MODEL
CONV_WIDTH = 3
N_GROUPS = 4
EXPERTS_PER_GROUP = 8
N_EXPERTS = N_GROUPS * EXPERTS_PER_GROUP
TOP_K_IN_GROUP = 2
EXPERT_FF = 512
MOE_BLOCK = 128
RMS_EPS = 1e-5
N_ATTN_LAYERS = (DEPTH + 1) // 2
N_CONV_LAYERS = DEPTH // 2

kernel_name = "hybrid_swa_shortconv_hmoe"

def rms_norm(x, g):
    xf = x.astype(jnp.float32)
    y = xf * lax.rsqrt(jnp.mean(xf * xf, axis=-1, keepdims=True) + RMS_EPS)
    return (y * g.astype(jnp.float32)).astype(x.dtype)

def t5_causal_bucket(dist):
    max_exact = N_REL_BUCKETS // 2
    d = jnp.maximum(dist, max_exact).astype(jnp.float32)
    large = max_exact + (jnp.log(d / max_exact) / math.log(REL_MAX_DISTANCE / max_exact)
                         * (N_REL_BUCKETS - max_exact)).astype(jnp.int32)
    large = jnp.minimum(large, N_REL_BUCKETS - 1)
    return jnp.where(dist < max_exact, dist, large)

def sliding_window_attention(h, w_qkv, b_qkv, w_o, b_o, sinks, rel_bias):
    B, S, _ = h.shape
    G = N_Q_HEADS // N_KV_HEADS
    qkv = h @ w_qkv + b_qkv
    q, k, v = jnp.split(qkv, [N_Q_HEADS * HEAD_DIM, (N_Q_HEADS + N_KV_HEADS) * HEAD_DIM], axis=-1)
    q = q.reshape(B, S, N_KV_HEADS, G, HEAD_DIM) * (HEAD_DIM ** -0.5)
    k = k.reshape(B, S, N_KV_HEADS, HEAD_DIM)
    v = v.reshape(B, S, N_KV_HEADS, HEAD_DIM)
    pad = jnp.zeros((B, ATTN_BLOCK, N_KV_HEADS, HEAD_DIM), h.dtype)
    k_pad = jnp.concatenate([pad, k], axis=1)
    v_pad = jnp.concatenate([pad, v], axis=1)
    n_blocks = S // ATTN_BLOCK
    q_blocks = q.reshape(B, n_blocks, ATTN_BLOCK, N_KV_HEADS, G, HEAD_DIM).transpose(1, 0, 2, 3, 4, 5)
    qi = jnp.arange(ATTN_BLOCK)[:, None]
    kj = jnp.arange(2 * ATTN_BLOCK)[None, :]
    dist = qi + ATTN_BLOCK - kj
    in_window = (dist >= 0) & (dist < WINDOW)
    bucket = t5_causal_bucket(jnp.maximum(dist, 0))
    bias = rel_bias[bucket].astype(jnp.float32)
    bias = bias.transpose(2, 0, 1).reshape(N_KV_HEADS, G, ATTN_BLOCK, 2 * ATTN_BLOCK)
    sink = sinks.astype(jnp.float32).reshape(N_KV_HEADS, G)[:, :, None, None]

    def one_block(args):
        n, qb = args
        kb = lax.dynamic_slice_in_dim(k_pad, n * ATTN_BLOCK, 2 * ATTN_BLOCK, axis=1)
        vb = lax.dynamic_slice_in_dim(v_pad, n * ATTN_BLOCK, 2 * ATTN_BLOCK, axis=1)
        s = jnp.einsum('bqhgd,bkhd->bhgqk', qb, kb).astype(jnp.float32) + bias
        valid = in_window & ((n - 1) * ATTN_BLOCK + kj >= 0)
        s = jnp.where(valid, s, -1e30)
        m = jnp.maximum(jnp.max(s, axis=-1, keepdims=True), sink)
        p = jnp.exp(s - m)
        denom = jnp.sum(p, axis=-1, keepdims=True) + jnp.exp(sink - m)
        p = (p / denom).astype(vb.dtype)
        return jnp.einsum('bhgqk,bkhd->bqhgd', p, vb)

    o = lax.map(one_block, (jnp.arange(n_blocks), q_blocks))
    o = o.transpose(1, 0, 2, 3, 4, 5).reshape(B, S, N_Q_HEADS * HEAD_DIM)
    return o @ w_o + b_o

def gated_short_conv(h, w_in, conv_w, w_out):
    S = h.shape[1]
    b_gate, c_gate, u = jnp.split(h @ w_in, 3, axis=-1)
    z = c_gate * u
    zp = jnp.pad(z, ((0, 0), (CONV_WIDTH - 1, 0), (0, 0)))
    conv = zp[:, 0:S] * conv_w[0]
    for j in range(1, CONV_WIDTH):
        conv = conv + zp[:, j:j + S] * conv_w[j]
    return (b_gate * conv) @ w_out

def hierarchical_moe(h, w_group, b_group, w_expert, b_expert, w_gate_up, w_down):
    B, S, D = h.shape
    T = B * S
    xt = h.reshape(T, D)
    group_probs = jax.nn.softmax((xt @ w_group + b_group).astype(jnp.float32), axis=-1)
    g_prob, g_idx = lax.top_k(group_probs, 1)
    exp_logits = (xt @ w_expert + b_expert).astype(jnp.float32).reshape(T, N_GROUPS, EXPERTS_PER_GROUP)
    sel = jnp.broadcast_to(g_idx[:, :, None], (T, 1, EXPERTS_PER_GROUP))
    in_group = jnp.take_along_axis(exp_logits, sel, axis=1)[:, 0]
    e_prob, e_local = lax.top_k(jax.nn.softmax(in_group, axis=-1), TOP_K_IN_GROUP)
    e_prob = e_prob / jnp.sum(e_prob, axis=-1, keepdims=True)
    gates = g_prob * e_prob
    expert_ids = g_idx * EXPERTS_PER_GROUP + e_local

    N = T * TOP_K_IN_GROUP
    flat_e = expert_ids.reshape(N)
    flat_tok = jnp.repeat(jnp.arange(T, dtype=jnp.int32), TOP_K_IN_GROUP)
    flat_gate = gates.reshape(N)
    order = jnp.argsort(flat_e)
    sorted_e = flat_e[order]
    counts = jnp.zeros((N_EXPERTS,), jnp.int32).at[flat_e].add(1)
    padded = (counts + MOE_BLOCK - 1) // MOE_BLOCK * MOE_BLOCK
    start = jnp.cumsum(counts) - counts
    pend = jnp.cumsum(padded)
    pstart = pend - padded
    dest = pstart[sorted_e] + jnp.arange(N, dtype=jnp.int32) - start[sorted_e]
    capacity = -(-N // MOE_BLOCK) * MOE_BLOCK + N_EXPERTS * MOE_BLOCK
    slot_tok = jnp.full((capacity,), T, jnp.int32).at[dest].set(flat_tok[order])
    slot_gate = jnp.zeros((capacity,), jnp.float32).at[dest].set(flat_gate[order])
    n_blk = capacity // MOE_BLOCK
    blk_start = jnp.arange(n_blk, dtype=jnp.int32) * MOE_BLOCK
    blk_expert = jnp.minimum(jnp.searchsorted(pend, blk_start, side='right'), N_EXPERTS - 1)
    x_pad = jnp.concatenate([xt, jnp.zeros((1, D), xt.dtype)], axis=0)
    xs = x_pad[slot_tok].reshape(n_blk, MOE_BLOCK, D)

    def expert_block(args):
        xb, e = args
        g, u = jnp.split(xb @ w_gate_up[e], 2, axis=-1)
        return (jax.nn.silu(g) * u) @ w_down[e]

    ys = lax.map(expert_block, (xs, blk_expert)).reshape(capacity, D)
    out = jax.ops.segment_sum(ys * slot_gate[:, None].astype(ys.dtype), slot_tok, num_segments=T + 1)[:T]
    return out.reshape(B, S, D)

def setup_inputs(seed: int = 0) -> dict:
    key = jax.random.key(seed)
    ks = jax.random.split(key, 24)
    f32 = jnp.float32
    nrm = lambda k, shape, s: (jax.random.normal(k, shape, f32) * s)
    D = D_MODEL
    return {
        "x": nrm(ks[0], (BATCH, SEQ, D), 1.0),
        "norm_mix": 1.0 + nrm(ks[1], (DEPTH, D), 0.02),
        "norm_ffn": 1.0 + nrm(ks[2], (DEPTH, D), 0.02),
        "final_norm": 1.0 + nrm(ks[3], (D,), 0.02),
        "rel_bias": nrm(ks[4], (N_REL_BUCKETS, N_Q_HEADS), 0.5),
        "attn_w_qkv": nrm(ks[5], (N_ATTN_LAYERS, D, QKV_DIM), D ** -0.5),
        "attn_b_qkv": nrm(ks[6], (N_ATTN_LAYERS, QKV_DIM), 0.02),
        "attn_w_o": nrm(ks[7], (N_ATTN_LAYERS, N_Q_HEADS * HEAD_DIM, D), (N_Q_HEADS * HEAD_DIM) ** -0.5),
        "attn_b_o": nrm(ks[8], (N_ATTN_LAYERS, D), 0.02),
        "attn_sinks": nrm(ks[9], (N_ATTN_LAYERS, N_Q_HEADS), 1.0),
        "conv_w_in": nrm(ks[10], (N_CONV_LAYERS, D, 3 * CONV_DIM), D ** -0.5),
        "conv_w": nrm(ks[11], (N_CONV_LAYERS, CONV_WIDTH, CONV_DIM), CONV_WIDTH ** -0.5),
        "conv_w_out": nrm(ks[12], (N_CONV_LAYERS, CONV_DIM, D), CONV_DIM ** -0.5),
        "moe_w_group": nrm(ks[13], (DEPTH, D, N_GROUPS), D ** -0.5),
        "moe_b_group": nrm(ks[14], (DEPTH, N_GROUPS), 0.01),
        "moe_w_expert": nrm(ks[15], (DEPTH, D, N_EXPERTS), D ** -0.5),
        "moe_b_expert": nrm(ks[16], (DEPTH, N_EXPERTS), 0.01),
        "moe_w_gate_up": nrm(ks[17], (DEPTH, N_EXPERTS, D, 2 * EXPERT_FF), D ** -0.5),
        "moe_w_down": nrm(ks[18], (DEPTH, N_EXPERTS, EXPERT_FF, D), EXPERT_FF ** -0.5),
    }

def reference(x, norm_mix, norm_ffn, final_norm, rel_bias, attn_w_qkv, attn_b_qkv, attn_w_o,
              attn_b_o, attn_sinks, conv_w_in, conv_w, conv_w_out, moe_w_group, moe_b_group,
              moe_w_expert, moe_b_expert, moe_w_gate_up, moe_w_down):
    h = x
    for i in range(DEPTH):
        xn = rms_norm(h, norm_mix[i])
        if i % N_MIXERS == 0:
            a = i // N_MIXERS
            mix = sliding_window_attention(xn, attn_w_qkv[a], attn_b_qkv[a], attn_w_o[a],
                                           attn_b_o[a], attn_sinks[a], rel_bias)
        else:
            c = i // N_MIXERS
            mix = gated_short_conv(xn, conv_w_in[c], conv_w[c], conv_w_out[c])
        h = h + mix
        h = h + hierarchical_moe(rms_norm(h, norm_ffn[i]), moe_w_group[i], moe_b_group[i],
                                 moe_w_expert[i], moe_b_expert[i], moe_w_gate_up[i], moe_w_down[i])
    return rms_norm(h, final_norm)


_drawn_inputs = setup_inputs


def setup_inputs(seed=0):
    import zlib

    import numpy as np

    out = dict(_drawn_inputs(seed))
    spreads = {}
    factors = {}
    for name, (base, spread) in spreads.items():
        noise = np.random.default_rng([zlib.crc32(name.encode()), seed]).standard_normal(out[name].shape)
        drawn = base * np.exp(spread * noise) if base else spread * noise
        out[name] = __import__('jax').numpy.asarray(drawn.astype(out[name].dtype))
    for name, factor in factors.items():
        out[name] = (out[name] * factor).astype(out[name].dtype)
    return out
```

```python
from contextlib import ExitStack

import concourse.bass as bass
from concourse import mybir

P = 128
F32R = mybir.dt.float32r
F32 = mybir.dt.float32
I32 = mybir.dt.int32
U32 = mybir.dt.uint32
ALU = mybir.AluOpType
ACT = mybir.ActivationFunctionType
X = mybir.AxisListType.X

BLOCK = 64
BIG_SLOTS = 2
SMALL_SLOTS = 2
RMS_EPS = 1e-5
MASKED = -1e30
PAD = -3e38
WINDOW = 128
BUCKETS = 32
ARENA = 13056
MAX_DIST = 128


def bucket_bounds():
    import math
    import numpy as np
    exact = BUCKETS // 2
    d = np.arange(WINDOW)
    far = exact + (np.log(np.maximum(d, exact).astype(np.float32) / exact) / math.log(MAX_DIST / exact)
                   * (BUCKETS - exact)).astype(np.int32)
    b = np.where(d < exact, d, np.minimum(far, BUCKETS - 1))
    return [(k, int(d[b == k].min()), int(d[b == k].max())) for k in range(BUCKETS) if (b == k).any()]


def build_trunk(nc, x, norm_mix, norm_ffn, final_norm, rel_bias, w_qkv, b_qkv, w_o, b_o, sinks,
                w_in, conv_w, w_out, w_group, b_group, w_expert, b_expert, w_gate_up, w_down, out):
    _, T, D = x.shape
    TT, DT = T // P, D // P
    L, E = w_gate_up.shape[0], w_gate_up.shape[1]
    FF = w_down.shape[2]
    FT = FF // P
    NG = w_group.shape[2]
    EG = E // NG
    H = sinks.shape[1]
    HD = 64
    KV = (w_qkv.shape[2] - H * HD) // (2 * HD)
    HG = H // KV
    NR = NG + E
    ROUNDS = T // BLOCK
    HALF = D // 2
    PAIRS = E // 2
    NONE = 2 * T

    with ExitStack() as ctx:
        def sb(name, shape, dt=F32):
            return ctx.enter_context(nc.sbuf_tensor(name, shape, dt))

        def sem(name):
            return ctx.enter_context(nc.semaphore(name))

        ctx.enter_context(nc.allow_non_contiguous_dma(reason="small parameters, once"))

        shared = {"big": [P, BIG_SLOTS, DT, D],
                  "small": [P, SMALL_SLOTS, FT, D],
                  "xr": [P, TT, D],
                  "xt": [P, DT, T],
                  "arena": [P, ARENA]}
        with ExitStack() as first:
            plain = {k: first.enter_context(nc.sbuf_tensor(k, shape, F32)) for k, shape in shared.items()}
        rounded = {k: sb(k + "_parts", shape, F32R) for k, shape in shared.items()}
        big, small, xr, xt, arena = (plain[k] for k in shared)
        h = sb("h", [P, TT, D])
        gain = sb("gain", [P, D])
        ident = sb("ident", [P, P])
        flip = sb("flip", [P, P])
        upper = sb("upper", [P, P])
        ones = sb("ones", [P, P])
        iota = sb("iota", [P, BLOCK])
        base = sb("base", [P, TT])
        wr = sb("wr", [P, DT, NR])
        br = sb("br", [P, NR])
        logitsT = sb("logitsT", [P, T])
        fold = sb("fold", [P, NR])
        eps = sb("eps", [P, 1])
        ss = sb("ss", [P, TT])
        rstd = sb("rstd", [P, TT])
        rank = sb("rank", [P, TT, E])
        dest = sb("dest", [P, TT, E])
        gate1 = sb("gate1", [P, TT])
        gate2 = sb("gate2", [P, TT])
        fullest = sb("fullest", [P, 1], I32)
        ps = [ctx.enter_context(nc.psum_tensor(f"ps{i}", [P, 512], F32)) for i in range(8)]

        toeplitz = nc.dram_tensor("toeplitz", [H, 3 * P], F32, kind="Internal").ap()
        rows_dram = [nc.dram_tensor(f"rows{l}", [2 * NONE, HALF], F32, kind="Internal").ap() for l in range(L)]

        class Carve:
            def __init__(self):
                self.at = 0

            def __call__(self, *shape):
                n = 1
                for s in shape:
                    n *= s
                a = arena[:, self.at:self.at + n]
                self.at += n
                assert self.at <= ARENA, self.at
                if len(shape) == 1:
                    return a
                names = "abcd"[:len(shape)]
                return a.rearrange(f"p ({' '.join(names)}) -> p {' '.join(names)}",
                                   **{k: s for k, s in zip(names[1:], shape[1:])})

        cut = Carve()
        bias = cut(KV, HG, 2 * P)
        scores = cut(2, HG, 2 * P)
        probsT = cut(HG, 2, P)
        o_flat = cut(D)
        keys = cut(KV, T)
        values = cut(TT, KV * HD)
        bq = cut(DT)
        bk = cut(1)
        bv = cut(KV * HD)
        sink = cut(KV, HG)
        peak = cut(2, HG)
        sums = cut(2, HG)
        sink_e = cut(2, HG)
        rden = cut(2, HG)
        toe = probsT.rearrange("p a b c -> p (a b c)")[:, 0:3 * P]
        relT = probsT.rearrange("p a b c -> p (a b c)")[:, 3 * P:3 * P + BUCKETS]
        bo = o_flat
        bias_rev = scores.rearrange("p a b c -> p (a b c)")
        squared = keys.rearrange("p a b -> p (a b)")
        qT = xr[:].rearrange("p a (b c) -> p (a b) c", c=T)
        def parts(a):
            return bass.AP(tensor=rounded[a.tensor.name], offset=a.offset, ap=[list(x) for x in a.ap])

        xt_low = xr[:].rearrange("p t (d c) -> p d t c", c=P)
        spare = small[:].rearrange("p s a b -> p (s a b)")
        cut = Carve()
        c_gate = cut(2, T)
        z = cut(2, T + 2)
        conv = cut(T)
        gated = cut(DT, T)
        gated_low = cut(DT, T)
        cw = cut(3, DT)
        cut = Carve()
        rt = cut(TT, 256)
        before = cut(TT, E)
        sel = cut(TT, 2, BLOCK)
        dcol = cut(TT, 2)
        xg = cut(DT, 2 * BLOCK)
        silu = cut(2, FF)
        hid = cut(2, FF)
        hidT = cut(2, FT, BLOCK)
        y_rows = cut(2, HALF)
        where_f = cut(2)
        where = cut(2).bitcast(I32)
        late = cut(2, 2, D)
        early = xt[:].rearrange("p (a k b) c -> p a k (b c)", a=2, k=2)
        stage = [early[:, 0], early[:, 1], late[:, 0], late[:, 1]]
        assert L == 2 and T == 512 and D == 1024 and HG == 8 and KV == 2

        x_in = [sem(f"x_in{t}") for t in range(TT)]
        rows_done = sem("rows_done")
        consts_ready = sem("consts_ready")
        pe_mark = sem("pe_mark")
        pool_mark = sem("pool_mark")
        dve_mark = sem("dve_mark")
        sp_mark = sem("sp_mark")
        pool_step = sem("pool_step")
        act_step = sem("act_step")
        dve_step = sem("dve_step")
        gain_in = sem("gain_in")
        router_in = [sem(f"router_in{l}") for l in range(L)]
        attn_in = sem("attn_in")
        rel_in = sem("rel_in")
        conv_in = [sem(f"conv_in{b}") for b in range(2)]
        w_out_in = sem("w_out_in")
        big_in = [sem(f"big_in{s}") for s in range(BIG_SLOTS)]
        small_in = [sem(f"small_in{s}") for s in range(SMALL_SLOTS)]
        h_ready = sem("h_ready")
        squares = sem("squares")
        xt_high = sem("xt_high")
        w_high = sem("w_high")
        w_split = sem("w_split")
        root_ready = sem("root_ready")
        xr_ready = sem("xr_ready")
        xt_ps = sem("xt_ps")
        keys_ready = sem("keys_ready")
        xt_even = sem("xt_even")
        xt_odd = sem("xt_odd")
        toe_ready = sem("toe_ready")
        toe_out = sem("toe_out")
        bias_in = sem("bias_in")
        flip_ps = sem("flip_ps")
        bias_ready = sem("bias_ready")
        qk_ps = sem("qk_ps")
        qk_ready = sem("qk_ready")
        score_ps = sem("score_ps")
        score_ready = sem("score_ready")
        peak_ready = sem("peak_ready")
        probs_ready = sem("probs_ready")
        sink_ready = sem("sink_ready")
        pT_ps = sem("pT_ps")
        pT_ready = sem("pT_ready")
        o_ps = sem("o_ps")
        o_ready = sem("o_ready")
        oT_ps = sem("oT_ps")
        oT_ready = sem("oT_ready")
        mix_ps = sem("mix_ps")
        mix_used = sem("mix_used")
        gates_ps = sem("gates_ps")
        c_ready = sem("c_ready")
        conv_ready = sem("conv_ready")
        halves_ps = sem("halves_ps")
        halves_ready = sem("halves_ready")
        before_ready = sem("before_ready")
        logits_ps = sem("logits_ps")
        shift_ready = sem("shift_ready")
        exp_ready = sem("exp_ready")
        mask_ready = sem("mask_ready")
        rank_ps = sem("rank_ps")
        route_ready = sem("route_ready")
        rows_in = [sem(f"rows_in{t}") for t in range(TT)]
        out_done = sem("out_done")

        class Stage:
            def __init__(self, tag):
                self.selected = sem(f"selected_{tag}")
                self.gathered = sem(f"gathered_{tag}")
                self.xg_ready = sem(f"xg_ready_{tag}")
                self.where_ready = sem(f"where_ready_{tag}")
                self.gu_done = sem(f"gu_done_{tag}")
                self.silu_ready = sem(f"silu_ready_{tag}")
                self.hid_ready = sem(f"hid_ready_{tag}")
                self.turned = sem(f"turned_{tag}")
                self.hidT_ready = sem(f"hidT_ready_{tag}")
                self.down_done = sem(f"down_done_{tag}")
                self.row_ready = [sem(f"row_ready{j}_{tag}") for j in range(2)]
                self.scattered = [sem(f"scattered{j}_{tag}") for j in range(2)]

        main = [Stage(f"m{l}") for l in range(L)]
        over = [Stage(f"o{l}") for l in range(L)]
        round_ready = [sem(f"round_ready{l}") for l in range(L)]
        over_in = [sem(f"over_in{l}") for l in range(L)]

        QUARTERS = 4
        QC = D // QUARTERS
        BIG_EXPERT = [2, 2 + E + QUARTERS + 1]
        BIG_CONV = 2 + E
        SMALL_EXPERT = [1, 1 + E]

        def big_slot(n):
            return n % BIG_SLOTS

        def small_slot(n):
            return n % SMALL_SLOTS

        def big_loaded(eng, n, more=0):
            own = sum(big_slot(m) == big_slot(n) for m in range(BIG_CONV, BIG_CONV + QUARTERS + 1) if m < n)
            eng.wait_ge(big_in[big_slot(n)], 16 * (n // BIG_SLOTS + 1 - own) + 16 * more)

        def small_loaded(eng, n, more=0):
            eng.wait_ge(small_in[small_slot(n)], 16 * (n // SMALL_SLOTS + 1) + 16 * more)

        CONV_W = DT * 3 * P

        def conv_weights(j):
            q = j * P // QC
            w = big[:, big_slot(BIG_CONV + q)].rearrange("p a b -> p (a b)")[:, 0:DT * 3 * QC].rearrange(
                "p (a n) -> p a n", n=QC)[:, :, j * P - q * QC:(j + 1) * P - q * QC]
            return w, spare[:, j % 2 * CONV_W:(j % 2 + 1) * CONV_W].rearrange("p (a n) -> p a n", n=P)

        def out_weights(k):
            at = 2 * CONV_W + k * D if k < 2 else (k - 2) * D
            return big[:, big_slot(BIG_CONV + QUARTERS), k, :], spare[:, at:at + D]

        def out_weights_wait(eng, k):
            if k >= 2:
                eng.wait_ge(gates_ps, DT - 1 if k < 5 else DT)

        block = ctx.enter_context(nc.Block())

        @block.sync
        def _(sp):
            def load_big(n, src, dst):
                sp.dma_start(dst, src).then_inc(big_in[big_slot(n)], 16)

            def load_small(n, src, dst):
                sp.dma_start(dst, src).then_inc(small_in[small_slot(n)], 16)

            def load_experts_over(l):
                sp.wait_ge(route_ready, l + 1)
                most = sp.value_load(fullest[0:1, 0:1], min_val=0, max_val=T)
                with sp.If(most > BLOCK):
                    with sp.Fori(1, ROUNDS) as r:
                        with sp.If(most > r * BLOCK):
                            with sp.Fori(0, PAIRS) as i:
                                sp.wait_ge(over[l].selected, r * PAIRS + i + (1 - PAIRS))
                                for j in range(2):
                                    e = bass.ds(i * 2 + j, 1)
                                    sp.dma_start(big[:, j], w_gate_up[l, e, :, :].rearrange(
                                        "a (k p) n -> p (a k) n", p=P)).then_inc(over_in[l], 16)
                                    sp.dma_start(small[:, j], w_down[l, e, :, :].rearrange(
                                        "a (k p) n -> p (a k) n", p=P)).then_inc(over_in[l], 16)
                            sp.wait_ge(over[l].down_done, r * E)
                            sp.sem_inc(sp_mark, 1)
                        with sp.Else():
                            sp.nop()
                        sp.nop()
                    sp.nop()
                with sp.Else():
                    sp.nop()
                sp.nop()

            def load_pair(l, es, big_free, small_free):
                for j in range(2):
                    n = BIG_EXPERT[l] + j
                    sp.wait_ge(*big_free[j])
                    load_big(n, w_gate_up[l, es[j], :, :].rearrange("a (k p) n -> p (a k) n", p=P),
                             big[:, big_slot(n)])
                for j in range(2):
                    n = SMALL_EXPERT[l] + j
                    if small_free[j]:
                        sp.wait_ge(*small_free[j])
                    load_small(n, w_down[l, es[j], :, :].rearrange("a (k p) n -> p (a k) n", p=P),
                               small[:, small_slot(n)])

            def load_experts(l, big_free, small_free):
                load_pair(l, [slice(0, 1), slice(1, 2)], big_free, small_free)
                with sp.Fori(1, PAIRS) as i:
                    load_pair(l, [bass.ds(i * 2 + j, 1) for j in range(2)],
                              [(main[l].gu_done, i * 2 - 1 + j) for j in range(2)],
                              [(main[l].down_done, i * 2 - 1 + j) for j in range(2)])

            def load_rows(l):
                sp.wait_ge(rows_done, l + 1)
                for t in range(TT):
                    sp.dma_start(stage[t], rows_dram[l].rearrange("(k t p c) d -> t p k (c d)", k=2, p=P, c=2)[t])\
                        .then_inc(rows_in[t], 16)

            for t in range(TT):
                sp.dma_start(h[:, t, :], x[0, t * P:(t + 1) * P, :]).then_inc(x_in[t], 16)
            sp.wait_ge(toe_ready, 1)
            sp.dma_start(toeplitz, toe[0:H, :]).then_inc(toe_out, 16)
            load_big(0, w_qkv[0, :, 0:H * HD].rearrange("(k p) n -> p k n", p=P), big[:, 0])
            sp.wait_ge(toe_out, 16)
            sp.dma_start(bias_rev.rearrange("p (h c) -> p h c", h=H),
                         bass.AP(tensor=toeplitz.tensor, offset=0, ap=[[1, P], [3 * P, H], [1, 2 * P]]))\
                .then_inc(bias_in, 16)
            load_small(0, w_qkv[0, :, H * HD:].rearrange("(k p) n -> p k n", p=P),
                       small[:, 0].rearrange("p a b -> p (a b)")[:, 0:DT * 2 * KV * HD]
                       .rearrange("p (k n) -> p k n", k=DT))
            load_big(1, w_o[0].rearrange("(k p) n -> p k n", p=P), big[:, 1])
            load_experts(0, [(qk_ps, DT), (mix_ps, 2 * TT)], [None, (qk_ps, DT + 2)])
            load_experts_over(0)
            for q in range(QUARTERS):
                n = BIG_CONV + q
                if q == 1:
                    load_rows(0)
                dst = big[:, big_slot(n)].rearrange("p a b -> p (a b)")[:, 0:DT * 3 * QC].rearrange(
                    "p (k g n) -> p k g n", k=DT, g=3)
                if q < BIG_SLOTS:
                    sp.wait_ge(main[0].gu_done, E - BIG_SLOTS + q + 1)
                else:
                    sp.wait_ge(gates_ps, (q - BIG_SLOTS + 1) * QC // P)
                for g in range(3):
                    sp.dma_start(dst[:, :, g, :], w_in[0, :, g * D + q * QC:g * D + (q + 1) * QC]
                                 .rearrange("(k p) n -> p k n", p=P)).then_inc(conv_in[q % 2], 16)
            n = BIG_CONV + QUARTERS
            sp.wait_ge(gates_ps, (QUARTERS - BIG_SLOTS + 1) * QC // P)
            sp.dma_start(big[:, big_slot(n)], w_out[0].rearrange("(k p) n -> p k n", p=P)).then_inc(w_out_in, 16)
            load_experts(1, [(gates_ps, DT), (mix_ps, 4 * TT)],
                         [(mix_ps, 4 * TT), (mix_ps, 4 * TT)])
            load_experts_over(1)
            load_rows(1)
            for t in range(TT):
                sp.wait_ge(xr_ready, 4 * TT + t + 1)
                sp.dma_start(out[0, t * P:(t + 1) * P, :], xr[:, t, :]).then_inc(out_done, 16)
            sp.wait_ge(out_done, 16 * TT)

        @block.gpsimd
        def _(pool):
            nc.gpsimd.memset(ident[:], 0.0).then_inc(pool_step, 1)
            nc.gpsimd.memset(ones[:], 1.0).then_inc(pool_step, 1)
            nc.gpsimd.memset(flip[:], 0.0).then_inc(pool_step, 1)
            nc.gpsimd.memset(eps[:], RMS_EPS).then_inc(consts_ready, 1)
            nc.gpsimd.iota(iota[:], [[1, BLOCK]], base=0, channel_multiplier=0,
                           allow_small_or_imprecise_dtypes=True).then_inc(consts_ready, 1)
            nc.gpsimd.iota(base[:], [[-P, TT]], base=NONE, channel_multiplier=-1,
                           allow_small_or_imprecise_dtypes=True).then_inc(consts_ready, 1)
            pool.wait_ge(pool_step, 3)
            nc.gpsimd.affine_select(out=ident[:], in_=ident[:], compare_op=ALU.not_equal, fill=1.0,
                                    base=0, pattern=[[-1, P]], channel_multiplier=1).then_inc(consts_ready, 1)
            nc.gpsimd.affine_select(out=flip[:], in_=flip[:], compare_op=ALU.not_equal, fill=1.0,
                                    base=1 - P, pattern=[[1, P]], channel_multiplier=1).then_inc(consts_ready, 1)
            nc.gpsimd.affine_select(out=upper[:], in_=ones[:], compare_op=ALU.is_gt, fill=0.0,
                                    base=0, pattern=[[1, P]], channel_multiplier=-1).then_inc(consts_ready, 1)
            nc.gpsimd.memset(logitsT[:], 0.0).then_inc(consts_ready, 1)

            def scatter(S, l, j, i):
                pool.wait_ge(S.row_ready[j], i + 1)
                pool.sem_inc(pool_mark, 1)
                nc.gpsimd.indirect_dma_start(
                    out=rows_dram[l], out_offset=bass.IndirectOffsetOnAxis(ap=where[:, j:j + 1], axis=0),
                    in_=y_rows[:, j, :], in_offset=None,
                    bounds_check=2 * NONE - 1, oob_is_err=False).then_inc(S.scattered[j], 16)

            for l in range(L):
                S = main[l]
                with pool.Fori(0, PAIRS) as i:
                    for j in range(2):
                        scatter(S, l, j, i)
                pool.wait_ge(route_ready, l + 1)
                most = pool.value_load(fullest[0:1, 0:1], min_val=0, max_val=T)
                with pool.If(most > BLOCK):
                    with pool.Fori(1, ROUNDS) as r:
                        with pool.If(most > r * BLOCK):
                            with pool.Fori(0, PAIRS) as i:
                                for j in range(2):
                                    scatter(over[l], l, j, r * PAIRS + i - PAIRS)
                                for j in range(2):
                                    pool.wait_ge(over[l].scattered[j], (r * PAIRS + i + (1 - PAIRS)) * 16)
                        with pool.Else():
                            pool.nop()
                        pool.nop()
                    pool.nop()
                with pool.Else():
                    pool.nop()
                for j in range(2):
                    pool.wait_ge(S.scattered[j], 16 * PAIRS)
                pool.sem_inc(rows_done, 1)

        @block.scalar
        def _(act):
            steps = [0]

            def load_gain(i):
                src = [norm_mix[0:1, :], norm_ffn[0:1, :], norm_mix[1:2, :], norm_ffn[1:2, :],
                       final_norm.rearrange("(a d) -> a d", a=1)][i]
                act.dma_start(gain[:], src.to_broadcast([P, D])).then_inc(gain_in, 16)

            def load_router(l):
                act.dma_start(wr[:, :, 0:NG], w_group[l].rearrange("(k p) n -> p k n", p=P)).then_inc(router_in[l], 16)
                act.dma_start(wr[:, :, NG:NR], w_expert[l].rearrange("(k p) n -> p k n", p=P)).then_inc(router_in[l], 16)
                act.dma_start(br[:, 0:NG], b_group[l:l + 1, :].to_broadcast([P, NG])).then_inc(router_in[l], 16)
                act.dma_start(br[:, NG:NR], b_expert[l:l + 1, :].to_broadcast([P, E])).then_inc(router_in[l], 16)

            def root(i, t):
                if i == 0:
                    act.wait_ge(x_in[t], 16)
                elif i % 2 == 1:
                    act.wait_ge(mix_used, TT * (i - 1) + 2 * t + 2)
                else:
                    act.wait_ge(h_ready, TT * (i // 2 - 1) + t + 1)
                nc.scalar.activation(squared, h[:, t, :], ACT.Square, accum_out=ss[:, t:t + 1]).then_inc(squares, 1)
                act.wait_ge(squares, TT * i + t + 1)
                if i > 0:
                    act.wait_ge(xr_ready, TT * (i - 1) + t + 1)
                nc.scalar.activation(rstd[:, t:t + 1], ss[:, t:t + 1], ACT.Sqrt,
                                     bias=eps[:], scale=1.0 / D).then_inc(root_ready, 1)

            def take_turned(i, t):
                if i == 2:
                    if t == 0:
                        act.wait_ge(h_ready, 2)
                    for half in range(2):
                        act.wait_ge(xt_ps, 8 * i + 2 * t + half + 1)
                        nc.scalar.activation(parts(xt[:, 4 * half:4 * half + 4, t * P:(t + 1) * P]),
                                             ps[(2 * t + half) % 4][:].rearrange("p (a b) -> p a b", b=P), ACT.Copy)\
                            .then_inc(xt_high, 1)
                    return
                act.wait_ge(xt_ps, 8 * i + 2 * t + 1)
                nc.scalar.activation(xt[:, 0:4, t * P:(t + 1) * P],
                                     ps[2 * t % 4][:].rearrange("p (a b) -> p a b", b=P), ACT.Copy).then_inc(xt_even, 1)

            def norm(i):
                for t in range(TT):
                    root(i, t)
                    if t >= 1 and i < 4:
                        take_turned(i, t - 1)
                if i < 4:
                    take_turned(i, TT - 1)
                    act.wait_ge(xr_ready, TT * (i + 1))
                    load_gain(i + 1)

            for g in range(KV):
                for p in range(2):
                    s0 = g * HG + p * 4
                    act.dma_start(relT[s0:s0 + 4, :], rel_bias[:, g * HG + p:g * HG + HG:2].rearrange("b h -> h b"))\
                        .then_inc(rel_in, 16)
            load_gain(0)
            for g in range(KV):
                for p in range(2):
                    act.dma_start(sink[:, g, p * 4:p * 4 + 4],
                                  sinks[0:1, g * HG + p:g * HG + HG:2].to_broadcast([P, 4])).then_inc(attn_in, 16)
            act.dma_start(bq, b_qkv[0, 0:H * HD].rearrange("(j p) -> p j", p=P)).then_inc(attn_in, 16)
            act.dma_start(bk, b_qkv[0, H * HD:(H + KV) * HD].rearrange("(p a) -> p a", a=1)).then_inc(attn_in, 16)
            act.dma_start(bv, b_qkv[0:1, (H + KV) * HD:].to_broadcast([P, KV * HD])).then_inc(attn_in, 16)
            act.dma_start(bo, b_o[0:1, :].to_broadcast([P, D])).then_inc(attn_in, 16)
            load_router(0)
            act.wait_ge(consts_ready, 7)
            norm(0)
            act.wait_ge(qk_ready, DT + 1)
            nc.scalar.activation(keys[HD:P, 0, :], keys[0:HD, 0, :], ACT.Copy)
            nc.scalar.activation(keys[0:HD, 1, :], keys[HD:P, 1, :], ACT.Copy).then_inc(keys_ready, 1)
            def att_exp(u):
                b = u % 2
                act.wait_ge(peak_ready, u + 1)
                n = u // KV
                lo = P if n == 0 else 0
                nc.scalar.activation(sink_e[:, b, :], sink_e[:, b, :], ACT.Exp).then_inc(sink_ready, 1)
                for k in range(HG):
                    nc.scalar.activation(scores[:, b, k, lo:], scores[:, b, k, lo:], ACT.Exp,
                                         bias=peak[:, b, k:k + 1], accum_out=sums[:, b, k:k + 1])\
                        .then_inc(probs_ready, 1)

            def att_turn(u):
                for f in range(4):
                    act.wait_ge(pT_ps, 4 * u + f + 1)
                    nc.scalar.activation(probsT[:, 2 * f:2 * f + 2],
                                         ps[4 + f % 2][:].rearrange("p (a c q) -> p a c q", a=2, c=2),
                                         ACT.Copy).then_inc(pT_ready, 1)

            def att_take_out(n):
                for f in range(2):
                    act.wait_ge(oT_ps, 2 * n + f + 1)
                    nc.scalar.activation(xt[:, 4 * f:4 * f + 4, n * P:(n + 1) * P],
                                         ps[7][:].rearrange("p (a b) -> p a b", b=P), ACT.Copy).then_inc(oT_ready, 1)

            U = TT * KV
            for u in range(U):
                att_exp(u)
                if u % KV == 0 and u >= KV:
                    att_take_out(u // KV - 1)
                att_turn(u)
            att_take_out(TT - 1)

            def router(l):
                act.wait_ge(halves_ps, l + 1)
                nc.scalar.activation(logitsT[0:NR, :], ps[4][0:NR, :], ACT.Copy).then_inc(halves_ready, 1)
                act.wait_ge(shift_ready, 2 * l + 1)
                nc.scalar.activation(rt[:, :, 16:20], rt[:, :, 16:20], ACT.Exp).then_inc(exp_ready, 1)
                act.wait_ge(shift_ready, 2 * l + 2)
                nc.scalar.activation(rt[:, :, 20:21], rt[:, :, 20:21], ACT.Exp).then_inc(exp_ready, 1)

            def take(S, i):
                act.wait_ge(S.gathered, i + 1)
                for half in range(2):
                    ins = nc.scalar.activation(xg[:, 4 * half:4 * half + 4, :],
                                               ps[half][:].rearrange("p (a b) -> p a b", a=4), ACT.Copy)
                ins.then_inc(S.xg_ready, 1)

            def swish(S, n, j):
                act.wait_ge(S.gu_done, n + 1)
                nc.scalar.activation(silu[BLOCK:P, j, :], ps[2 + j][0:BLOCK, :], ACT.Silu).then_inc(S.silu_ready, 1)

            def take_hidden(S, n, j):
                act.wait_ge(S.turned, n + 1)
                nc.scalar.activation(hidT[:, j], ps[4 + j][:, 0:FT * BLOCK].rearrange("p (a b) -> p a b", a=FT),
                                     ACT.Copy).then_inc(S.hidT_ready, 1)

            def pair(S, i, last=False):
                swish(S, i * 2, 0)
                swish(S, i * 2 + 1, 1)
                take_hidden(S, i * 2, 0)
                if not last:
                    take(S, i + 1)
                take_hidden(S, i * 2 + 1, 1)

            def experts(l):
                S = main[l]
                take(S, 0)
                with act.Fori(0, PAIRS - 1) as i:
                    pair(S, i)
                pair(S, PAIRS - 1, last=True)
                act.wait_ge(route_ready, l + 1)
                most = act.value_load(fullest[0:1, 0:1], min_val=0, max_val=T)
                with act.If(most > BLOCK):
                    with act.Fori(1, ROUNDS) as r:
                        with act.If(most > r * BLOCK):
                            with act.Fori(0, PAIRS) as i:
                                q = r * PAIRS + i - PAIRS
                                take(over[l], q)
                                pair(over[l], q, last=True)
                        with act.Else():
                            act.nop()
                        act.nop()
                    act.nop()
                with act.Else():
                    act.nop()

            norm(1)
            router(0)
            experts(0)
            def split_conv(j):
                if j * P % QC == 0:
                    q = j * P // QC
                    act.wait_ge(conv_in[q % 2], 16 * 3 * (q // 2 + 1))
                if j >= 2:
                    act.wait_ge(gates_ps, j - 1)
                else:
                    act.wait_ge(rows_done, 1)
                w, high = conv_weights(j)
                nc.scalar.activation(parts(high), w, ACT.Copy).then_inc(w_high, 1)

            def split_out(ks):
                for k in ks:
                    out_weights_wait(act, k)
                    w, high = out_weights(k)
                    nc.scalar.activation(parts(high), w, ACT.Copy).then_inc(w_high, 1)

            split_conv(0)
            norm(2)
            for k in range(3):
                act.dma_start(cw[:, k, :], conv_w[0, k].rearrange("(j p) -> p j", p=P)).then_inc(router_in[1], 16)
            load_router(1)

            split_conv(1)
            for j in range(DT):
                act.wait_ge(gates_ps, j + 1)
                if j >= 2:
                    act.wait_ge(conv_ready, j - 1)
                nc.scalar.activation(c_gate[:, j % 2, :], ps[3 * (j % 2) + 1][:], ACT.Copy).then_inc(c_ready, 1)
                if j + 2 < DT:
                    split_conv(j + 2)
                if j == DT - 2:
                    act.wait_ge(w_out_in, 16)
                    split_out(range(5))
                if j == DT - 1:
                    split_out(range(5, DT))
            norm(3)
            router(1)
            experts(1)
            norm(4)

        @block.tensor
        def _(pe):
            def turn_tile(i, t):
                pe.wait_ge(xr_ready, TT * i + t + 1)
                for half in range(2):
                    f = 2 * t + half
                    if f >= 4:
                        pe.wait_ge(xt_odd if half else xt_even, TT * i + (f - 4) // 2 + 1)
                    for a in range(4):
                        d = half * 4 + a
                        mm = nc.tensor.transpose(ps[f % 4][:, a * P:(a + 1) * P],
                                                 xr[:, t, d * P:(d + 1) * P], ident[:])
                    mm.then_inc(xt_ps, 1)
                if t == TT - 1:
                    pe.wait_ge(xt_even, TT * (i + 1))
                    pe.wait_ge(xt_odd, TT * (i + 1))

            def turn(i):
                for t in range(TT):
                    turn_tile(i, t)

            pe.wait_ge(consts_ready, 7)
            turn(0)
            wq = big[:, 0]
            wkv = small[:, 0].rearrange("p a b -> p (a b)")[:, 0:DT * 2 * KV * HD].rearrange("p (k n) -> p k n", k=DT)
            big_loaded(pe, 0)
            for j in range(DT):
                bank = 4 + j % 2
                if j >= 2:
                    pe.wait_ge(qk_ready, j - 1)
                for k in range(DT):
                    mm = nc.tensor.matmul(ps[bank][:], wq[:, k, j * P:(j + 1) * P], xt[:, k, :],
                                          start=(k == 0), stop=(k == DT - 1))
                mm.then_inc(qk_ps, 1)
            pe.wait_ge(bias_in, 16)
            for f in range(8):
                if f >= 2:
                    pe.wait_ge(bias_ready, f - 1)
                nc.tensor.matmul(ps[6 + f % 2][:], flip[:], bias_rev[:, f * 512:(f + 1) * 512],
                                 start=True, stop=True).then_inc(flip_ps, 1)
            small_loaded(pe, 0)
            pe.wait_ge(qk_ready, DT - 1)
            for k in range(DT):
                mm = nc.tensor.matmul(ps[4][:], wkv[:, k, 0:KV * HD], xt[:, k, :],
                                      start=(k == 0), stop=(k == DT - 1))
            mm.then_inc(qk_ps, 1)
            pe.wait_ge(qk_ready, DT)
            for t in range(TT):
                for k in range(DT):
                    mm = nc.tensor.matmul(ps[5][:, t * P:(t + 1) * P], xt[:, k, t * P:(t + 1) * P],
                                          wkv[:, k, KV * HD:2 * KV * HD], start=(k == 0), stop=(k == DT - 1))
            mm.then_inc(qk_ps, 1)

            U = TT * KV

            def att_scores(u):
                n, g = u // KV, u % KV
                lo = 1 if n == 0 else 0
                for hh in range(HG):
                    if u >= 1 and hh % 4 == 0:
                        pe.wait_ge(score_ready, 8 * (u - 1) + hh + 4)
                    j, half = (g * HG + hh) // 2, hh % 2
                    slot = half * 4 + hh // 2
                    bank, col = slot // 2, (slot % 2) * 2 * P
                    r0 = half * HD
                    mm = nc.tensor.matmul(ps[bank][:, col + lo * P:col + 2 * P],
                                          qT[r0:r0 + HD, j, n * P:(n + 1) * P],
                                          keys[r0:r0 + HD, g, (n - 1 + lo) * P:(n + 1) * P],
                                          start=True, stop=True, skip_group_check=True)
                    if hh % 4 == 3:
                        mm.then_inc(score_ps, 1)

            def att_turn(u):
                n = u // KV
                for f in range(4):
                    pe.wait_ge(probs_ready, HG * u + 2 * f + 2)
                    if 4 * u + f >= 2:
                        pe.wait_ge(pT_ready, 4 * u + f - 1)
                    for a in range(2):
                        for c in range(2):
                            if n == 0 and c == 0:
                                continue
                            mm = nc.tensor.transpose(ps[4 + f % 2][:, (2 * a + c) * P:(2 * a + c + 1) * P],
                                                     scores[:, u % 2, 2 * f + a, c * P:(c + 1) * P], ident[:])
                    mm.then_inc(pT_ps, 1)

            def att_out(u):
                n, g = u // KV, u % KV
                if u >= 1:
                    pe.wait_ge(o_ready, u)
                first = 1 if n == 0 else 0
                for slot in range(HG):
                    if slot % 2 == 0:
                        pe.wait_ge(pT_ready, 4 * u + slot // 2 + 1)
                    hh = slot % 4 * 2 + slot // 4
                    for c in range(first, 2):
                        mm = nc.tensor.matmul(ps[6][:, hh * HD:(hh + 1) * HD], probsT[:, slot, c, :],
                                              values[:, n - 1 + c, g * HD:(g + 1) * HD],
                                              start=(c == first), stop=(c == 1))
                mm.then_inc(o_ps, 1)

            def att_turn_out(n):
                pe.wait_ge(o_ready, KV * (n + 1))
                for f in range(2):
                    if 2 * n + f >= 1:
                        pe.wait_ge(oT_ready, 2 * n + f)
                    for a in range(4):
                        mm = nc.tensor.transpose(ps[7][:, a * P:(a + 1) * P],
                                                 o_flat[:, (4 * f + a) * P:(4 * f + a + 1) * P], ident[:])
                    mm.then_inc(oT_ps, 1)

            pe.wait_ge(qk_ready, DT + 2)
            pe.wait_ge(keys_ready, 1)
            att_scores(0)
            for u in range(U):
                if u + 1 < U:
                    att_scores(u + 1)
                if u % KV == 0 and u >= KV:
                    att_turn_out(u // KV - 1)
                att_turn(u)
                att_out(u)
            att_turn_out(TT - 1)

            def split_product(bank, left, left_low, right, right_low, start, stop):
                for a, b in ((left, right), (left, right_low), (left_low, right)):
                    mm = nc.tensor.matmul(bank, parts(a), parts(b), start=start and a is left and b is right,
                                          stop=stop and a is left_low)
                return mm

            def project(first, i, product):
                for t in range(TT):
                    for ks in ([range(5), range(5, DT)] if t == 0 else [range(DT)]):
                        for half in range(2):
                            f = 2 * t + half
                            if f >= 2:
                                pe.wait_ge(mix_used, first + f - 1)
                            for k in ks:
                                mm = product(ps[6 + f % 2][:], t, half, k)
                            if k == DT - 1:
                                mm.then_inc(mix_ps, 1)
                    if t >= 1:
                        turn_tile(i, t - 1)
                turn_tile(i, TT - 1)

            pe.wait_ge(oT_ready, 2 * TT)
            pe.wait_ge(o_ready, U)
            big_loaded(pe, 1)

            def attention_product(bank, t, half, k):
                return nc.tensor.matmul(bank, xt[:, k, t * P:(t + 1) * P], big[:, 1, k, half * HALF:(half + 1) * HALF],
                                        start=(k == 0), stop=(k == DT - 1))

            project(0, 1, attention_product)

            def router(l):
                pe.wait_ge(router_in[l], 16 * (4 + (3 if l else 0)))
                for k in range(DT // 2):
                    for half in range(2):
                        d = half * DT // 2 + k
                        mm = nc.tensor.matmul(ps[4][half * BLOCK:half * BLOCK + NR, :], wr[:, d, :], xt[:, d, :],
                                              start=(k == 0), stop=(k == DT // 2 - 1))
                mm.then_inc(halves_ps, 1)
                pe.wait_ge(halves_ready, 2 * l + 2)
                for t in range(TT):
                    mm = nc.tensor.matmul(ps[7][:, t * NR:(t + 1) * NR], logitsT[:, t * P:(t + 1) * P], fold[:],
                                          start=True, stop=True)
                mm.then_inc(logits_ps, 1)
                pe.wait_ge(mask_ready, l + 1)
                nc.tensor.matmul(ps[5][:, 0:TT * E], upper[:], rt[:, :, 224:256], start=True, stop=False)
                pe.wait_ge(before_ready, l + 1)
                nc.tensor.matmul(ps[5][:, E:TT * E], ones[:], before[:, 0:TT - 1, :], start=False, stop=True)
                nc.tensor.matmul(ps[5][:, TT * E:(TT + 1) * E], ones[:], before[:, TT - 1, :],
                                 start=True, stop=True).then_inc(rank_ps, 1)

            def gather(S, i):
                pe.wait_ge(S.selected, i + 1)
                for d in range(DT):
                    for t in range(TT):
                        mm = nc.tensor.matmul(ps[d // 4][:, (d % 4) * P:(d % 4 + 1) * P], xr[:, t, d * P:(d + 1) * P],
                                              sel[:, t, :, :], start=(t == 0), stop=(t == TT - 1))
                for t in range(TT):
                    mm = nc.tensor.matmul(ps[4][:, 0:2], sel[:, t, :, :], dcol[:, t, :],
                                          start=(t == 0), stop=(t == TT - 1))
                mm.then_inc(S.gathered, 1)

            def gate_up(S, j, w):
                for k in range(DT):
                    for half in range(2):
                        mm = nc.tensor.matmul(ps[2 + j][half * BLOCK:(half + 1) * BLOCK, :],
                                              xg[:, k, j * BLOCK:(j + 1) * BLOCK], w[:, k, half * FF:(half + 1) * FF],
                                              start=(k == 0), stop=(k == DT - 1))
                mm.then_inc(S.gu_done, 1)

            def turn_hidden(S, n, j):
                pe.wait_ge(S.hid_ready, n + 1)
                pe.sem_inc(pe_mark, 1)
                for k in range(FT):
                    mm = nc.tensor.transpose(ps[4 + j][:, k * BLOCK:(k + 1) * BLOCK],
                                             hid[BLOCK:P, j, k * P:(k + 1) * P], ident[BLOCK:P, BLOCK:P])
                mm.then_inc(S.turned, 1)

            def down(S, n, j, w):
                pe.wait_ge(S.hidT_ready, n + 1)
                for k in range(FT):
                    for half in range(2):
                        mm = nc.tensor.matmul(ps[6 + j][half * BLOCK:(half + 1) * BLOCK, :], hidT[:, j, k, :],
                                              w[:, k, half * HALF:(half + 1) * HALF],
                                              start=(k == 0), stop=(k == FT - 1))
                mm.then_inc(S.down_done, 1)

            def experts(l):
                S = main[l]
                b0, s0 = BIG_EXPERT[l], SMALL_EXPERT[l]
                gather(S, 0)

                def pair(i, last=False):
                    for j in range(2):
                        big_loaded(pe, b0 + j, i)
                        if j == 0:
                            pe.wait_ge(S.xg_ready, i + 1)
                        gate_up(S, j, big[:, big_slot(b0 + j)])
                    pe.wait_ge(S.where_ready, i + 1)
                    turn_hidden(S, i * 2, 0)
                    small_loaded(pe, s0, i)
                    down(S, i * 2, 0, small[:, small_slot(s0)])
                    if not last:
                        gather(S, i + 1)
                    turn_hidden(S, i * 2 + 1, 1)
                    small_loaded(pe, s0 + 1, i)
                    down(S, i * 2 + 1, 1, small[:, small_slot(s0 + 1)])

                pair(0)
                with pe.Fori(1, PAIRS - 1) as i:
                    pair(i)
                pair(PAIRS - 1, last=True)
                pe.wait_ge(route_ready, l + 1)
                most = pe.value_load(fullest[0:1, 0:1], min_val=0, max_val=T)
                with pe.If(most > BLOCK):
                    with pe.Fori(1, ROUNDS) as r:
                        with pe.If(most > r * BLOCK):
                            with pe.Fori(0, PAIRS) as i:
                                q = r * PAIRS + i - PAIRS
                                gather(over[l], q)
                                pe.wait_ge(over[l].xg_ready, q + 1)
                                pe.wait_ge(over[l].where_ready, q + 1)
                                pe.wait_ge(over_in[l], (r * PAIRS + i + (1 - PAIRS)) * 64)
                                for j in range(2):
                                    gate_up(over[l], j, big[:, j])
                                for j in range(2):
                                    turn_hidden(over[l], q * 2 + j, j)
                                    down(over[l], q * 2 + j, j, small[:, j])
                        with pe.Else():
                            pe.nop()
                        pe.nop()
                    pe.nop()
                with pe.Else():
                    pe.nop()

            router(0)
            experts(0)
            turn(2)
            for j in range(DT):
                w, high = conv_weights(j)
                pe.wait_ge(w_split, j + 1)
                if j >= 2:
                    pe.wait_ge(conv_ready, j - 1)
                for g in range(3):
                    for k in range(DT):
                        mm = split_product(ps[3 * (j % 2) + g][:], high[:, 3 * k + g, :], w[:, 3 * k + g, :],
                                           xt[:, k, :], xt_low[:, k], k == 0, k == DT - 1)
                mm.then_inc(gates_ps, 1)

            def conv_product(bank, t, half, k):
                if t == 0 and half == 0:
                    pe.wait_ge(w_split, DT + k + 1)
                w, high = out_weights(k)
                cols = slice(half * HALF, (half + 1) * HALF)
                rows = slice(t * P, (t + 1) * P)
                return split_product(bank, gated[:, k, rows], gated_low[:, k, rows], high[:, cols], w[:, cols],
                                     k == 0, k == DT - 1)

            pe.wait_ge(conv_ready, DT)
            project(2 * TT, 3, conv_product)
            router(1)
            experts(1)

        @block.vector
        def _(dve):
            steps = [0]
            V = nc.vector

            def step(ins):
                ins.then_inc(dve_step, 1)
                steps[0] += 1
                dve.wait_ge(dve_step, steps[0])

            def norm_tile(i, t):
                dve.wait_ge(root_ready, TT * i + t + 1)
                step(V.reciprocal(rstd[:, t:t + 1], rstd[:, t:t + 1]))
                if t == 0:
                    dve.wait_ge(gain_in, 16 * (i + 1))
                V.scalar_tensor_tensor(out=xr[:, t, :], in0=h[:, t, :], scalar=rstd[:, t:t + 1],
                                       in1=gain[:], op0=ALU.mult, op1=ALU.mult).then_inc(xr_ready, 1)

            def take_turned(i, t):
                if i == 2:
                    for half in range(2):
                        dve.wait_ge(xt_high, 2 * t + half + 1)
                        ds = slice(4 * half, 4 * half + 4)
                        V.tensor_tensor(parts(xt_low[:, ds, t]), ps[(2 * t + half) % 4][:].rearrange(
                            "p (a b) -> p a b", b=P), parts(xt[:, ds, t * P:(t + 1) * P]), ALU.subtract)\
                            .then_inc(xt_odd if half else xt_even, 1)
                    return
                dve.wait_ge(xt_ps, 8 * i + 2 * t + 2)
                V.tensor_copy(xt[:, 4:8, t * P:(t + 1) * P],
                              ps[(2 * t + 1) % 4][:].rearrange("p (a b) -> p a b", b=P)).then_inc(xt_odd, 1)

            def norm(i, produce, ahead=False):
                if ahead:
                    produce(0)
                for t in range(TT):
                    if not ahead:
                        produce(t)
                    elif t + 1 < TT:
                        produce(t + 1)
                    norm_tile(i, t)
                    if t >= 1 and i < 4:
                        take_turned(i, t - 1)
                if i < 4:
                    take_turned(i, TT - 1)

            step(V.memset(toe[0:H, :], MASKED))
            dve.wait_ge(rel_in, 16 * 4)
            bounds = bucket_bounds()
            for k, (b, lo, hi) in enumerate(bounds):
                x0, x1 = 2 * P - 1 - hi, 2 * P - lo
                ins = V.tensor_copy(toe[0:H, x0:x1], relT[0:H, b:b + 1].to_broadcast([H, x1 - x0]))
            ins.then_inc(toe_ready, 1)
            norm(0, lambda t: dve.wait_ge(x_in[t], 16))
            step(V.tensor_tensor(fold[:], ident[:, 0:NR], ident[:, BLOCK:BLOCK + NR], ALU.add))
            dve.wait_ge(attn_in, 16 * 8)
            for j in range(DT):
                dve.wait_ge(qk_ps, j + 1)
                V.tensor_scalar(qT[:, j, :], ps[4 + j % 2][:], bq[:, j:j + 1], HD ** -0.5,
                                ALU.add, ALU.mult).then_inc(qk_ready, 1)
            for f in range(8):
                dve.wait_ge(flip_ps, f + 1)
                V.tensor_copy(bias.rearrange("p a b c -> p (a b c)")[:, f * 512:(f + 1) * 512],
                              ps[6 + f % 2][:]).then_inc(bias_ready, 1)
            dve.wait_ge(qk_ps, DT + 1)
            for g in range(KV):
                half = slice(g * HD, (g + 1) * HD)
                ins = V.tensor_scalar(keys[half, g, :], ps[4][half, :], bk[half, :], None, ALU.add)
            ins.then_inc(qk_ready, 1)
            for t in range(TT):
                ins = V.tensor_tensor(h[:, t, :], h[:, t, :], bo, ALU.add)
            step(ins)
            dve.wait_ge(qk_ps, DT + 2)
            V.tensor_tensor(values, ps[5][:].rearrange("p (t n) -> p t n", t=TT),
                            bv.unsqueeze(1).to_broadcast([P, TT, KV * HD]), ALU.add).then_inc(qk_ready, 1)
            dve.wait_ge(bias_ready, 8)

            U = TT * KV

            def att_bias(u):
                n, g, b = u // KV, u % KV, u % 2
                lo = P if n == 0 else 0
                if u >= 2:
                    dve.wait_ge(pT_ps, 4 * (u - 1))
                for hh in range(HG):
                    if hh % 4 == 0:
                        dve.wait_ge(score_ps, 2 * u + hh // 4 + 1)
                    k = (hh % 2) * 4 + hh // 2
                    ins = V.tensor_tensor_reduce(scores[:, b, k, lo:], ps[k // 2][:, (k % 2) * 2 * P + lo:(k % 2 + 1) * 2 * P],
                                                 bias[:, g, k, lo:], 1.0, PAD, ALU.add, ALU.max, peak[:, b, k:k + 1])
                    ins.then_inc(score_ready, 1)
                dve.wait_ge(score_ready, HG * (u + 1))
                step(V.tensor_tensor(peak[:, b, :], peak[:, b, :], sink[:, g, :], ALU.max))
                step(V.tensor_scalar(peak[:, b, :], peak[:, b, :], -1.0, None, ALU.mult))
                V.tensor_tensor(sink_e[:, b, :], sink[:, g, :], peak[:, b, :], ALU.add).then_inc(peak_ready, 1)

            def att_rest(u):
                n, g, b = u // KV, u % KV, u % 2
                dve.wait_ge(probs_ready, HG * (u + 1))
                dve.wait_ge(sink_ready, u + 1)
                step(V.tensor_tensor(rden[:, b, :], sums[:, b, :], sink_e[:, b, :], ALU.add))
                step(V.reciprocal(rden[:, b, :], rden[:, b, :]))
                dve.wait_ge(o_ps, u + 1)
                if n >= 1:
                    dve.wait_ge(oT_ps, 2 * n)
                for half in range(2):
                    ins = V.tensor_tensor(
                        o_flat[:, g * 512:(g + 1) * 512].rearrange("p (i a d) -> p a i d", a=2, d=HD)[:, half],
                        ps[6][:].rearrange("p (i a d) -> p a i d", a=2, d=HD)[:, half],
                        rden[:, b, half * 4:half * 4 + 4].unsqueeze(2).to_broadcast([P, 4, HD]), ALU.mult)
                ins.then_inc(o_ready, 1)

            att_bias(0)
            for u in range(U):
                if u + 1 < U:
                    att_bias(u + 1)
                att_rest(u)

            def add_mix(l):
                def add(t):
                    for half in range(2):
                        f = 2 * t + half
                        dve.wait_ge(mix_ps, 2 * TT * l + f + 1)
                        hs = h[:, t, half * HALF:(half + 1) * HALF]
                        V.tensor_tensor(hs, ps[6 + f % 2][:], hs, ALU.add).then_inc(mix_used, 1)
                    dve.wait_ge(mix_used, 2 * TT * l + 2 * t + 2)
                return add

            def add_rows(l):
                def add(t):
                    dve.wait_ge(rows_in[t], 16 * (l + 1))
                    step(V.scalar_tensor_tensor(out=h[:, t, :], in0=stage[t][:, 0, :], scalar=gate1[:, t:t + 1],
                                                in1=h[:, t, :], op0=ALU.mult, op1=ALU.add))
                    V.scalar_tensor_tensor(out=h[:, t, :], in0=stage[t][:, 1, :], scalar=gate2[:, t:t + 1],
                                           in1=h[:, t, :], op0=ALU.mult, op1=ALU.add).then_inc(h_ready, 1)
                    dve.wait_ge(h_ready, TT * l + t + 1)
                return add

            def router(l):
                lg = rt[:, :, 32:32 + NR]
                gp, gm = rt[:, :, 0:8], rt[:, :, 8:16]
                eg = rt[:, :, 16:20]
                p2 = rt[:, :, 20:21]
                og = rt[:, :, 24:28]
                gi = rt[:, :, 28:29]
                i1, i2 = rt[:, :, 29:30], rt[:, :, 30:31]
                prod = rt[:, :, 72:104]
                ig, em = rt[:, :, 104:112], rt[:, :, 112:120]
                idx = rt[:, :, 120:128].bitcast(U32)
                gs, s2 = rt[:, :, 128:129], rt[:, :, 129:130]
                m2 = rt[:, :, 192:224]
                m12 = rt[:, :, 224:256]
                io = iota[:, 0:E].unsqueeze(1).to_broadcast([P, TT, E])
                V.memset(gp, PAD)
                dve.wait_ge(halves_ps, l + 1)
                V.tensor_copy(logitsT[BLOCK:BLOCK + NR, :], ps[4][BLOCK:BLOCK + NR, :]).then_inc(halves_ready, 1)
                dve.wait_ge(logits_ps, l + 1)
                step(V.tensor_tensor(lg, ps[7][:, 0:TT * NR].rearrange("p (t n) -> p t n", t=TT),
                                     br[:].unsqueeze(1).to_broadcast([P, TT, NR]), ALU.add))
                step(V.tensor_copy(gp[:, :, 0:NG], lg[:, :, 0:NG]))
                for t in range(TT):
                    ins = V.max(gm[:, t, :], gp[:, t, :])
                step(ins)
                for t in range(TT):
                    V.max_index(idx[:, t, :], gm[:, t, :], gp[:, t, :])
                V.tensor_tensor(eg, lg[:, :, 0:NG], gm[:, :, 0:1].to_broadcast([P, TT, NG]),
                                ALU.subtract).then_inc(shift_ready, 1)
                dve.wait_ge(shift_ready, 2 * l + 1)
                step(V.tensor_copy(gi, idx[:, :, 0:1]))
                step(V.tensor_tensor(og, iota[:, 0:NG].unsqueeze(1).to_broadcast([P, TT, NG]),
                                     gi.to_broadcast([P, TT, NG]), ALU.is_equal))
                for t in range(TT):
                    ins = V.tensor_tensor(prod[:, t, :].rearrange("p (g j) -> p g j", g=NG),
                                          lg[:, t, NG:NR].rearrange("p (g j) -> p g j", g=NG),
                                          og[:, t, :].unsqueeze(2).to_broadcast([P, NG, EG]), ALU.mult)
                step(ins)
                for t in range(TT):
                    ins = V.tensor_reduce(ig[:, t, :], prod[:, t, :].rearrange("p (g j) -> p j g", g=NG), X, ALU.add)
                step(ins)
                for t in range(TT):
                    ins = V.max(em[:, t, :], ig[:, t, :])
                step(ins)
                for t in range(TT):
                    V.max_index(idx[:, t, :], em[:, t, :], ig[:, t, :])
                V.tensor_tensor(p2, em[:, :, 1:2], em[:, :, 0:1], ALU.subtract).then_inc(shift_ready, 1)
                dve.wait_ge(shift_ready, 2 * l + 2)
                step(V.tensor_copy(rt[:, :, 29:31], idx[:, :, 0:2]))
                step(V.scalar_tensor_tensor(out=rt[:, :, 29:31], in0=gi.to_broadcast([P, TT, 2]), scalar=float(EG),
                                            in1=rt[:, :, 29:31], op0=ALU.mult, op1=ALU.add))
                V.tensor_tensor(m2, io, i2.to_broadcast([P, TT, E]), ALU.is_equal)
                step(V.tensor_tensor(m12, io, i1.to_broadcast([P, TT, E]), ALU.is_equal))
                step(V.tensor_tensor(m12, m12, m2, ALU.add))
                dve.sem_inc(mask_ready, 1)
                V.tensor_copy(before[:, 0, :], m12[:, 0, :])
                step(V.tensor_tensor(before[:, 1, :], m12[:, 0, :], m12[:, 1, :], ALU.add))
                step(V.tensor_tensor(before[:, 2, :], before[:, 1, :], m12[:, 2, :], ALU.add))
                step(V.tensor_tensor(before[:, 3, :], before[:, 2, :], m12[:, 3, :], ALU.add))
                dve.sem_inc(before_ready, 1)
                V.scalar_tensor_tensor(out=dest[:], in0=m2, scalar=-float(T),
                                       in1=base[:].unsqueeze(2).to_broadcast([P, TT, E]), op0=ALU.mult, op1=ALU.add)
                dve.wait_ge(exp_ready, 2 * l + 2)
                step(V.tensor_reduce(gs, eg, X, ALU.add))
                step(V.scalar_tensor_tensor(out=s2, in0=p2, scalar=1.0, in1=gs, op0=ALU.add, op1=ALU.mult))
                step(V.reciprocal(gate1[:].unsqueeze(2), s2))
                V.tensor_tensor(gate2[:].unsqueeze(2), gate1[:].unsqueeze(2), p2, ALU.mult)
                dve.wait_ge(rank_ps, l + 1)
                step(V.scalar_tensor_tensor(out=rank[:], in0=ps[5][:, 0:TT * E].rearrange("p (t e) -> p t e", t=TT),
                                            scalar=1.0, in1=m12, op0=ALU.add, op1=ALU.mult))
                step(V.tensor_scalar(rank[:], rank[:], -1.0, None, ALU.add))
                select(main[l], slice(0, 2))
                V.tensor_reduce(rt[:, 0, 130:131], ps[5][:, TT * E:(TT + 1) * E], X, ALU.max).then_inc(dve_step, 1)
                steps[0] += 1
                dve.wait_ge(dve_step, steps[0])
                V.tensor_copy(fullest[:], rt[:, 0, 130:131]).then_inc(route_ready, 1)

            def select(S, pair_at):
                ranks = rank[:, :, pair_at]
                V.tensor_tensor(sel, iota[:].unsqueeze(1).unsqueeze(1).to_broadcast([P, TT, 2, BLOCK]),
                                ranks.unsqueeze(3).to_broadcast([P, TT, 2, BLOCK]), ALU.is_equal)
                V.tensor_copy(dcol, dest[:, :, pair_at]).then_inc(S.selected, 1)

            def hidden(S, n, j):
                dve.wait_ge(S.silu_ready, n + 1)
                V.tensor_tensor(hid[BLOCK:P, j, :], silu[BLOCK:P, j, :], ps[2 + j][BLOCK:P, :], ALU.mult)\
                    .then_inc(S.hid_ready, 1)

            def find_rows(S, i, taken=None):
                dve.wait_ge(S.gathered, i + 1)
                if taken is not None:
                    dve.wait_ge(S.row_ready[0], taken)
                for j in range(2):
                    for c in range(2):
                        ins = V.tensor_scalar(where_f[c * BLOCK:(c + 1) * BLOCK, j:j + 1],
                                              ps[4][j * BLOCK:(j + 1) * BLOCK, j:j + 1], -2.0, float(2 * NONE + c),
                                              ALU.mult, ALU.add)
                ins.then_inc(S.where_ready, 1)

            def take_rows(S, n, i, j, free=None):
                dve.wait_ge(S.down_done, n + 1)
                if j == 0:
                    dve.wait_ge(S.where_ready, i + 1)
                    if free is not None:
                        for b in range(2):
                            dve.wait_ge(S.scattered[b], free)
                    V.tensor_copy(where, where_f)
                V.tensor_copy(y_rows[:, j, :], ps[6 + j][:]).then_inc(S.row_ready[j], 1)

            def experts(l):
                S = main[l]
                find_rows(S, 0)

                def pair(i, free, last=False):
                    if not last:
                        select(S, bass.ds(i * 2 + 2, 2))
                    hidden(S, i * 2, 0)
                    hidden(S, i * 2 + 1, 1)
                    take_rows(S, i * 2, i, 0, free)
                    if not last:
                        find_rows(S, i + 1, i + 1)
                    take_rows(S, i * 2 + 1, i, 1)

                pair(0, None)
                with dve.Fori(1, PAIRS - 1) as i:
                    pair(i, i * 16)
                pair(PAIRS - 1, (PAIRS - 1) * 16, last=True)
                dve.wait_ge(route_ready, l + 1)
                most = dve.value_load(fullest[0:1, 0:1], min_val=0, max_val=T)
                with dve.If(most > BLOCK):
                    for j in range(2):
                        dve.wait_ge(S.scattered[j], 16 * PAIRS)
                    with dve.Fori(1, ROUNDS) as r:
                        with dve.If(most > r * BLOCK):
                            V.tensor_scalar(rank[:], rank[:], -float(BLOCK), None, ALU.add).then_inc(round_ready[l], 1)
                            dve.wait_ge(round_ready[l], r)
                            dve.sem_inc(dve_mark, 1)
                            with dve.Fori(0, PAIRS) as i:
                                q = r * PAIRS + i - PAIRS
                                select(over[l], bass.ds(i * 2, 2))
                                find_rows(over[l], q)
                                hidden(over[l], q * 2, 0)
                                hidden(over[l], q * 2 + 1, 1)
                                take_rows(over[l], q * 2, q, 0)
                                take_rows(over[l], q * 2 + 1, q, 1)
                                for j in range(2):
                                    dve.wait_ge(over[l].scattered[j], (q + 1) * 16)
                        with dve.Else():
                            dve.nop()
                        dve.nop()
                    dve.nop()
                with dve.Else():
                    dve.nop()

            norm(1, add_mix(0))
            router(0)
            experts(0)

            def split_low(n, w, high):
                dve.wait_ge(w_high, n + 1)
                V.tensor_tensor(parts(w), w, parts(high), ALU.subtract).then_inc(w_split, 1)

            split_low(0, *conv_weights(0))
            norm(2, add_rows(0), ahead=True)
            split_low(1, *conv_weights(1))
            for b in range(2):
                ins = V.memset(z[:, b, 0:2], 0.0)
            step(ins)
            dve.wait_ge(router_in[1], 16 * 7)
            for j in range(DT):
                b = j % 2
                dve.wait_ge(gates_ps, j + 1)
                dve.wait_ge(c_ready, j + 1)
                step(V.tensor_tensor(z[:, b, 2:T + 2], c_gate[:, b, :], ps[3 * b + 2][:], ALU.mult))
                step(V.tensor_scalar(conv, z[:, b, 0:T], cw[:, 0, j:j + 1], None, ALU.mult))
                for k in (1, 2):
                    step(V.scalar_tensor_tensor(out=conv, in0=z[:, b, k:T + k], scalar=cw[:, k, j:j + 1],
                                                in1=conv, op0=ALU.mult, op1=ALU.add))
                step(V.tensor_tensor(conv, conv, ps[3 * b][:], ALU.mult))
                step(V.tensor_copy(parts(gated[:, j, :]), conv))
                V.tensor_tensor(parts(gated_low[:, j, :]), conv, parts(gated[:, j, :]), ALU.subtract).then_inc(conv_ready, 1)
                dve.wait_ge(conv_ready, j + 1)
                if j + 2 < DT:
                    split_low(j + 2, *conv_weights(j + 2))
                for k in (range(5) if j == DT - 2 else range(5, DT) if j == DT - 1 else []):
                    split_low(DT + k, *out_weights(k))
            norm(3, add_mix(1))
            router(1)
            experts(1)
            norm(4, add_rows(1), ahead=True)


_INS = ['x', 'norm_mix', 'norm_ffn', 'final_norm', 'rel_bias', 'attn_w_qkv', 'attn_b_qkv', 'attn_w_o',
        'attn_b_o', 'attn_sinks', 'conv_w_in', 'conv_w', 'conv_w_out', 'moe_w_group', 'moe_b_group',
        'moe_w_expert', 'moe_b_expert', 'moe_w_gate_up', 'moe_w_down']
_OUT = ((1, 512, 1024), 'float32')


def kernel(**inputs):
    import numpy as _np
    import concourse.bacc as _bacc
    from concourse import mybir as _mybir
    from concourse.bass_utils import run_bass_kernel_spmd as _run

    nc = _bacc.Bacc("TRN2", target_bir_lowering=False, num_devices=1)
    arrays, args = {}, []
    for name in _INS:
        a = _np.ascontiguousarray(inputs[name])
        arrays[f"in_{name}_dram"] = a
        args.append(nc.dram_tensor(f"in_{name}_dram", a.shape, _mybir.dt.from_np(a.dtype), kind="ExternalInput").ap())
    args.append(nc.dram_tensor("out_dram", _OUT[0], _mybir.dt.from_np(_np.dtype(_OUT[1])), kind="ExternalOutput").ap())
    build_trunk(nc, *args)
    r = _run(nc, [arrays], core_ids=[0])
    return r.results[0]["out_dram"]
```

```python
from contextlib import ExitStack

import concourse.bass as bass
from concourse import mybir

P = 128
F32R = mybir.dt.float32r
F32 = mybir.dt.float32
I32 = mybir.dt.int32
U32 = mybir.dt.uint32
ALU = mybir.AluOpType
ACT = mybir.ActivationFunctionType
X = mybir.AxisListType.X

BLOCK = 64
BIG_SLOTS = 2
SMALL_SLOTS = 2
RMS_EPS = 1e-5
MASKED = -1e30
PAD = -3e38
WINDOW = 128
BUCKETS = 32
ARENA = 13056
MAX_DIST = 128


def bucket_bounds():
    import math
    import numpy as np
    exact = BUCKETS // 2
    d = np.arange(WINDOW)
    far = exact + (np.log(np.maximum(d, exact).astype(np.float32) / exact) / math.log(MAX_DIST / exact)
                   * (BUCKETS - exact)).astype(np.int32)
    b = np.where(d < exact, d, np.minimum(far, BUCKETS - 1))
    return [(k, int(d[b == k].min()), int(d[b == k].max())) for k in range(BUCKETS) if (b == k).any()]


def build_trunk(nc, x, norm_mix, norm_ffn, final_norm, rel_bias, w_qkv, b_qkv, w_o, b_o, sinks,
                w_in, conv_w, w_out, w_group, b_group, w_expert, b_expert, w_gate_up, w_down, out):
    _, T, D = x.shape
    TT, DT = T // P, D // P
    L, E = w_gate_up.shape[0], w_gate_up.shape[1]
    FF = w_down.shape[2]
    FT = FF // P
    NG = w_group.shape[2]
    EG = E // NG
    H = sinks.shape[1]
    HD = 64
    KV = (w_qkv.shape[2] - H * HD) // (2 * HD)
    HG = H // KV
    NR = NG + E
    ROUNDS = T // BLOCK
    HALF = D // 2
    PAIRS = E // 2
    LAST_CUTS = 4
    NONE = 2 * T

    with ExitStack() as ctx:
        def sb(name, shape, dt=F32):
            return ctx.enter_context(nc.sbuf_tensor(name, shape, dt))

        def sem(name):
            return ctx.enter_context(nc.semaphore(name))

        ctx.enter_context(nc.allow_non_contiguous_dma(reason="small parameters, once"))

        shared = {"big": [P, BIG_SLOTS, DT, D],
                  "small": [P, SMALL_SLOTS, FT, D],
                  "xr": [P, TT, D],
                  "xt": [P, DT, T],
                  "arena": [P, ARENA]}
        with ExitStack() as first:
            plain = {k: first.enter_context(nc.sbuf_tensor(k, shape, F32)) for k, shape in shared.items()}
        rounded = {k: sb(k + "_parts", shape, F32R) for k, shape in shared.items()}
        big, small, xr, xt, arena = (plain[k] for k in shared)
        h = sb("h", [P, TT, D])
        gain = sb("gain", [P, D])
        ident = sb("ident", [P, P])
        flip = sb("flip", [P, P])
        upper = sb("upper", [P, P])
        ones = sb("ones", [P, P])
        iota = sb("iota", [P, BLOCK])
        base = sb("base", [P, TT])
        wr = sb("wr", [P, DT, NR])
        br = sb("br", [P, NR])
        logitsT = sb("logitsT", [P, T])
        fold = sb("fold", [P, NR])
        eps = sb("eps", [P, 1])
        ss = sb("ss", [P, TT])
        rstd = sb("rstd", [P, TT])
        rank = sb("rank", [P, TT, E])
        dest = sb("dest", [P, TT, E])
        gate1 = sb("gate1", [P, TT])
        gate2 = sb("gate2", [P, TT])
        fullest = sb("fullest", [P, 1], I32)
        ps = [ctx.enter_context(nc.psum_tensor(f"ps{i}", [P, 512], F32)) for i in range(8)]

        toeplitz = nc.dram_tensor("toeplitz", [H, 3 * P], F32, kind="Internal").ap()
        rows_dram = [nc.dram_tensor(f"rows{l}", [2 * NONE, HALF], F32, kind="Internal").ap() for l in range(L)]

        class Carve:
            def __init__(self):
                self.at = 0

            def __call__(self, *shape):
                n = 1
                for s in shape:
                    n *= s
                a = arena[:, self.at:self.at + n]
                self.at += n
                assert self.at <= ARENA, self.at
                if len(shape) == 1:
                    return a
                names = "abcd"[:len(shape)]
                return a.rearrange(f"p ({' '.join(names)}) -> p {' '.join(names)}",
                                   **{k: s for k, s in zip(names[1:], shape[1:])})

        cut = Carve()
        bias = cut(KV, HG, 2 * P)
        scores = cut(2, HG, 2 * P)
        probsT = cut(HG, 2, P)
        bo = cut(D)
        keys = cut(KV, T)
        values = cut(TT, KV * HD)
        bq = cut(DT)
        bk = cut(1)
        bv = cut(1)
        sink = cut(KV, HG)
        peak = cut(3, HG)
        sums = cut(3, HG)
        sink_e = cut(3, HG)
        rden = cut(3, HG)
        toe = probsT.rearrange("p a b c -> p (a b c)")[:, 0:3 * P]
        relT = probsT.rearrange("p a b c -> p (a b c)")[:, 3 * P:3 * P + BUCKETS]
        valuesT = probsT.rearrange("p a b c -> p (a b c)")[:, 0:T]
        bias_rev = scores.rearrange("p a b c -> p (a b c)")
        squared = keys.rearrange("p a b -> p (a b)")
        def parts(a):
            return bass.AP(tensor=rounded[a.tensor.name], offset=a.offset, ap=[list(x) for x in a.ap])

        xt_low = xr[:].rearrange("p t (d c) -> p d t c", c=P)
        spare = small[:].rearrange("p s a b -> p (s a b)")
        cut = Carve()
        c_gate = cut(2, T)
        z = cut(2, T + 2)
        conv = cut(T)
        gated = cut(DT, T)
        gated_low = cut(DT, T)
        cw = cut(3, DT)
        cut = Carve()
        rt = cut(TT, 256)
        before = cut(TT, E)
        sel = cut(TT, 2, BLOCK)
        dcol = cut(TT, 2)
        xg = cut(DT, 2 * BLOCK)
        silu = cut(2, FF)
        hid = cut(2, FF)
        hidT = cut(2, FT, BLOCK)
        y_rows = cut(2, HALF)
        where_f = cut(2)
        where = cut(2).bitcast(I32)
        late = cut(2, 2, D)
        early = xt[:].rearrange("p (a k b) c -> p a k (b c)", a=2, k=2)
        stage = [early[:, 0], early[:, 1], late[:, 0], late[:, 1]]
        assert L == 2 and T == 512 and D == 1024 and HG == 8 and KV == 2

        x_in = [sem(f"x_in{t}") for t in range(TT)]
        rows_done = sem("rows_done")
        consts_ready = sem("consts_ready")
        pe_mark = sem("pe_mark")
        pool_mark = sem("pool_mark")
        dve_mark = sem("dve_mark")
        sp_mark = sem("sp_mark")
        pool_step = sem("pool_step")
        dve_step = sem("dve_step")
        gain_in = sem("gain_in")
        router_in = [sem(f"router_in{l}") for l in range(L)]
        attn_in = sem("attn_in")
        rel_in = sem("rel_in")
        conv_in = [sem(f"conv_in{b}") for b in range(2)]
        w_out_in = sem("w_out_in")
        last_in = [[sem(f"last_in{l}{q}") for q in range(LAST_CUTS)] for l in range(L)]
        big_in = [sem(f"big_in{s}") for s in range(BIG_SLOTS)]
        kv_in = sem("kv_in")
        down_in = [[sem(f"down_in{odd}{j}") for j in range(2)] for odd in range(2)]
        h_ready = sem("h_ready")
        squares = sem("squares")
        xt_high = sem("xt_high")
        w_high = sem("w_high")
        w_split = sem("w_split")
        root_ready = sem("root_ready")
        xr_ready = sem("xr_ready")
        xt_ps = sem("xt_ps")
        keys_ready = sem("keys_ready")
        xt_even = sem("xt_even")
        xt_odd = sem("xt_odd")
        toe_ready = sem("toe_ready")
        toe_out = sem("toe_out")
        bias_in = sem("bias_in")
        flip_ps = sem("flip_ps")
        bias_ready = sem("bias_ready")
        qk_ps = sem("qk_ps")
        qk_ready = sem("qk_ready")
        score_ps = sem("score_ps")
        score_ready = sem("score_ready")
        peak_ready = sem("peak_ready")
        probs_ready = sem("probs_ready")
        sink_ready = sem("sink_ready")
        pT_ps = sem("pT_ps")
        pT_ready = sem("pT_ready")
        o_ps = sem("o_ps")
        rden_ready = sem("rden_ready")
        scaled_dve = sem("scaled_dve")
        scaled_act = sem("scaled_act")
        wo_high = sem("wo_high")
        wo_split = sem("wo_split")
        valuesT_ready = sem("valuesT_ready")
        values_ps = sem("values_ps")
        oT_high = sem("oT_high")
        oT_ready = sem("oT_ready")
        mix_ps = sem("mix_ps")
        mix_used = sem("mix_used")
        gates_ps = sem("gates_ps")
        c_ready = sem("c_ready")
        conv_ready = sem("conv_ready")
        halves_ps = sem("halves_ps")
        halves_ready = sem("halves_ready")
        before_ready = sem("before_ready")
        logits_ps = sem("logits_ps")
        shift_ready = sem("shift_ready")
        exp_ready = sem("exp_ready")
        mask_ready = sem("mask_ready")
        rank_ps = sem("rank_ps")
        route_ready = sem("route_ready")
        rows_in = [sem(f"rows_in{t}") for t in range(TT)]
        out_done = sem("out_done")

        class Stage:
            def __init__(self, tag):
                self.selected = sem(f"selected_{tag}")
                self.gathered = sem(f"gathered_{tag}")
                self.xg_ready = sem(f"xg_ready_{tag}")
                self.where_ready = sem(f"where_ready_{tag}")
                self.gu_done = sem(f"gu_done_{tag}")
                self.silu_ready = sem(f"silu_ready_{tag}")
                self.hid_ready = sem(f"hid_ready_{tag}")
                self.turned = sem(f"turned_{tag}")
                self.hidT_ready = sem(f"hidT_ready_{tag}")
                self.down_done = sem(f"down_done_{tag}")
                self.row_ready = [sem(f"row_ready{j}_{tag}") for j in range(2)]
                self.scattered = [sem(f"scattered{j}_{tag}") for j in range(2)]

        main = [Stage(f"m{l}") for l in range(L)]
        over = [Stage(f"o{l}") for l in range(L)]
        round_ready = [sem(f"round_ready{l}") for l in range(L)]
        over_in = [sem(f"over_in{l}") for l in range(L)]

        QUARTERS = 4
        QC = D // QUARTERS
        BIG_EXPERT = [2, 2 + E + QUARTERS + 1]
        BIG_CONV = 2 + E

        def big_slot(n):
            return n % BIG_SLOTS

        def big_loaded(eng, n, more=0):
            own = sum(big_slot(m) == big_slot(n) for m in range(BIG_CONV - 1, BIG_CONV + QUARTERS + 1) if m < n)
            eng.wait_ge(big_in[big_slot(n)], 16 * (n // BIG_SLOTS + 1 - own) + 16 * more)

        def down_slot(odd, j):
            return (late.rearrange("p a b c -> p (a b) c"), xt[:].rearrange("p (a b) c -> p a (b c)", a=FT))[j] \
                if odd else small[:, j]

        def down_loaded(eng, l, i, odd, j):
            eng.wait_ge(down_in[odd][j], 16 * (i + 1 + l * PAIRS // 2))

        KV_SPLIT = DT
        CONV_SPLIT = DT + 1
        KV_W = DT * 2 * KV * HD

        def query_weights(j):
            return big[:, 0, :, j * P:(j + 1) * P], \
                spare[:, KV_W + j % 2 * D:KV_W + (j % 2 + 1) * D].rearrange("p (k n) -> p k n", n=P)

        def queries(n):
            return big[:, 0, n, :].rearrange("p (j c) -> p j c", c=P)

        def key_value_weights():
            return [spare[:, a:a + KV_W].rearrange("p (k n) -> p k n", k=DT) for a in (0, 2 * KV_W)]

        def mix_weights(k):
            return big[:, 1, k, :], spare[:, k * D:(k + 1) * D]

        unit_scores = [scores[:, 0], scores[:, 1], big[:, 0, TT:TT + 2, :].rearrange("p a (b c) -> p (a b) c", c=2 * P)]

        def turned_bank(u, f):
            return ps[(4, 5, 7)[(4 * u + f) % 3]]

        CONV_W = DT * 3 * P

        def conv_weights(j):
            q = j * P // QC
            w = big[:, big_slot(BIG_CONV + q)].rearrange("p a b -> p (a b)")[:, 0:DT * 3 * QC].rearrange(
                "p (a n) -> p a n", n=QC)[:, :, j * P - q * QC:(j + 1) * P - q * QC]
            return w, spare[:, j % 2 * CONV_W:(j % 2 + 1) * CONV_W].rearrange("p (a n) -> p a n", n=P)

        def out_weights(k):
            at = 2 * CONV_W + k * D if k < 2 else (k - 2) * D
            return big[:, big_slot(BIG_CONV + QUARTERS), k, :], spare[:, at:at + D]

        def out_weights_wait(eng, k):
            if k >= 2:
                eng.wait_ge(gates_ps, DT - 1 if k < 5 else DT)

        block = ctx.enter_context(nc.Block())

        @block.sync
        def _(sp):
            def load_big(n, src, dst):
                sp.dma_start(dst, src).then_inc(big_in[big_slot(n)], 16)

            def load_experts_over(l):
                sp.wait_ge(route_ready, l + 1)
                most = sp.value_load(fullest[0:1, 0:1], min_val=0, max_val=T)
                with sp.If(most > BLOCK):
                    with sp.Fori(1, ROUNDS) as r:
                        with sp.If(most > r * BLOCK):
                            with sp.Fori(0, PAIRS) as i:
                                sp.wait_ge(over[l].selected, r * PAIRS + i + (1 - PAIRS))
                                for j in range(2):
                                    e = bass.ds(i * 2 + j, 1)
                                    sp.dma_start(big[:, j], w_gate_up[l, e, :, :].rearrange(
                                        "a (k p) n -> p (a k) n", p=P)).then_inc(over_in[l], 16)
                                    sp.dma_start(small[:, j], w_down[l, e, :, :].rearrange(
                                        "a (k p) n -> p (a k) n", p=P)).then_inc(over_in[l], 16)
                            sp.wait_ge(over[l].down_done, r * E)
                            sp.sem_inc(sp_mark, 1)
                        with sp.Else():
                            sp.nop()
                        sp.nop()
                    sp.nop()
                with sp.Else():
                    sp.nop()
                sp.nop()

            def load_up(l, es, free):
                for j in range(2):
                    n = BIG_EXPERT[l] + j
                    sp.wait_ge(*free[j])
                    load_big(n, w_gate_up[l, es[j], :, :].rearrange("a (k p) n -> p (a k) n", p=P),
                             big[:, big_slot(n)])

            def load_down(l, es, odd, free):
                for j in range(2):
                    sp.wait_ge(*free[j])
                    sp.dma_start(down_slot(odd, j), w_down[l, es[j], :, :].rearrange("a (k p) n -> p (a k) n", p=P))\
                        .then_inc(down_in[odd][j], 16)

            def load_experts(l, big_free, small_free):
                def experts_of(i):
                    return [bass.ds(i * 2 + j, 1) for j in range(2)]

                def after_up(i):
                    return [(main[l].gu_done, i * 2 - 1 + j) for j in range(2)]

                def after_down(i):
                    return [(main[l].down_done, i * 2 - 3 + j) for j in range(2)]

                load_up(l, [slice(0, 1), slice(1, 2)], big_free)
                load_down(l, [slice(0, 1), slice(1, 2)], 0, small_free)
                load_down(l, [slice(2, 3), slice(3, 4)], 1, [(mix_ps, 2 * TT * (l + 1)), (halves_ps, l + 1)])
                with sp.Fori(0, PAIRS // 2 - 1) as i:
                    for odd in range(2):
                        load_up(l, experts_of(i * 2 + (1 + odd)), after_up(i * 2 + (1 + odd)))
                        load_down(l, experts_of(i * 2 + (2 + odd)), odd, after_down(i * 2 + (2 + odd)))
                free = after_up(PAIRS - 1)
                sp.wait_ge(*free[0])
                n = BIG_EXPERT[l] + E - 2
                load_big(n, w_gate_up[l, E - 2].rearrange("(k p) n -> p k n", p=P), big[:, big_slot(n)])
                sp.wait_ge(*free[1])
                for q in range(LAST_CUTS):
                    ks = slice(q * DT // LAST_CUTS, (q + 1) * DT // LAST_CUTS)
                    sp.dma_start(big[:, big_slot(n + 1), ks], w_gate_up[l, E - 1].rearrange(
                        "(k p) n -> p k n", p=P)[:, ks]).then_inc(last_in[l][q], 16)

            def load_rows(l):
                sp.wait_ge(rows_done, l + 1)
                for t in range(TT):
                    sp.dma_start(stage[t], rows_dram[l].rearrange("(k t p c) d -> t p k (c d)", k=2, p=P, c=2)[t])\
                        .then_inc(rows_in[t], 16)

            for t in range(TT):
                sp.dma_start(h[:, t, :], x[0, t * P:(t + 1) * P, :]).then_inc(x_in[t], 16)
            sp.wait_ge(toe_ready, 1)
            sp.dma_start(toeplitz, toe[0:H, :]).then_inc(toe_out, 16)
            load_big(0, w_qkv[0, :, 0:H * HD].rearrange("(k p) n -> p k n", p=P), big[:, 0])
            sp.wait_ge(toe_out, 16)
            sp.dma_start(bias_rev.rearrange("p (h c) -> p h c", h=H),
                         bass.AP(tensor=toeplitz.tensor, offset=0, ap=[[1, P], [3 * P, H], [1, 2 * P]]))\
                .then_inc(bias_in, 16)
            sp.dma_start(key_value_weights()[0], w_qkv[0, :, H * HD:].rearrange("(k p) n -> p k n", p=P))\
                .then_inc(kv_in, 16)
            load_big(1, w_o[0].rearrange("(k p) n -> p k n", p=P), big[:, 1])
            load_experts(0, [(pT_ps, 4 * TT * KV), (mix_ps, 2 * TT)], [(mix_ps, 2 * TT), (mix_ps, 2 * TT)])
            load_experts_over(0)
            for q in range(QUARTERS):
                n = BIG_CONV + q
                if q == 1:
                    load_rows(0)
                dst = big[:, big_slot(n)].rearrange("p a b -> p (a b)")[:, 0:DT * 3 * QC].rearrange(
                    "p (k g n) -> p k g n", k=DT, g=3)
                if q < BIG_SLOTS:
                    sp.wait_ge(main[0].gu_done, E - BIG_SLOTS + q + 1)
                else:
                    sp.wait_ge(gates_ps, (q - BIG_SLOTS + 1) * QC // P)
                for g in range(3):
                    sp.dma_start(dst[:, :, g, :], w_in[0, :, g * D + q * QC:g * D + (q + 1) * QC]
                                 .rearrange("(k p) n -> p k n", p=P)).then_inc(conv_in[q % 2], 16)
            n = BIG_CONV + QUARTERS
            sp.wait_ge(gates_ps, (QUARTERS - BIG_SLOTS + 1) * QC // P)
            sp.dma_start(big[:, big_slot(n)], w_out[0].rearrange("(k p) n -> p k n", p=P)).then_inc(w_out_in, 16)
            load_experts(1, [(gates_ps, DT), (mix_ps, 4 * TT)],
                         [(mix_ps, 4 * TT), (mix_ps, 4 * TT)])
            load_experts_over(1)
            load_rows(1)
            for t in range(TT):
                sp.wait_ge(xr_ready, 4 * TT + t + 1)
                sp.dma_start(out[0, t * P:(t + 1) * P, :], xr[:, t, :]).then_inc(out_done, 16)
            sp.wait_ge(out_done, 16 * TT)

        @block.gpsimd
        def _(pool):
            nc.gpsimd.memset(ident[:], 0.0).then_inc(pool_step, 1)
            nc.gpsimd.memset(ones[:], 1.0).then_inc(pool_step, 1)
            nc.gpsimd.memset(flip[:], 0.0).then_inc(pool_step, 1)
            nc.gpsimd.memset(eps[:], RMS_EPS).then_inc(consts_ready, 1)
            nc.gpsimd.iota(iota[:], [[1, BLOCK]], base=0, channel_multiplier=0,
                           allow_small_or_imprecise_dtypes=True).then_inc(consts_ready, 1)
            nc.gpsimd.iota(base[:], [[-P, TT]], base=NONE, channel_multiplier=-1,
                           allow_small_or_imprecise_dtypes=True).then_inc(consts_ready, 1)
            pool.wait_ge(pool_step, 3)
            nc.gpsimd.affine_select(out=ident[:], in_=ident[:], compare_op=ALU.not_equal, fill=1.0,
                                    base=0, pattern=[[-1, P]], channel_multiplier=1).then_inc(consts_ready, 1)
            nc.gpsimd.affine_select(out=flip[:], in_=flip[:], compare_op=ALU.not_equal, fill=1.0,
                                    base=1 - P, pattern=[[1, P]], channel_multiplier=1).then_inc(consts_ready, 1)
            nc.gpsimd.affine_select(out=upper[:], in_=ones[:], compare_op=ALU.is_gt, fill=0.0,
                                    base=0, pattern=[[1, P]], channel_multiplier=-1).then_inc(consts_ready, 1)
            nc.gpsimd.memset(logitsT[:], 0.0).then_inc(consts_ready, 1)

            big_loaded(pool, 1)
            pool.wait_ge(qk_ps, DT + 2)
            for k in range(DT):
                w, high = mix_weights(k)
                nc.gpsimd.tensor_copy(parts(high), w).then_inc(wo_high, 1)
                pool.wait_ge(wo_high, k + 1)
                nc.gpsimd.tensor_tensor(parts(w), w, parts(high), ALU.subtract).then_inc(wo_split, 1)

            def scatter(S, l, j, i):
                pool.wait_ge(S.row_ready[j], i + 1)
                pool.sem_inc(pool_mark, 1)
                nc.gpsimd.indirect_dma_start(
                    out=rows_dram[l], out_offset=bass.IndirectOffsetOnAxis(ap=where[:, j:j + 1], axis=0),
                    in_=y_rows[:, j, :], in_offset=None,
                    bounds_check=2 * NONE - 1, oob_is_err=False).then_inc(S.scattered[j], 16)

            for l in range(L):
                S = main[l]
                with pool.Fori(0, PAIRS) as i:
                    for j in range(2):
                        scatter(S, l, j, i)
                pool.wait_ge(route_ready, l + 1)
                most = pool.value_load(fullest[0:1, 0:1], min_val=0, max_val=T)
                with pool.If(most > BLOCK):
                    with pool.Fori(1, ROUNDS) as r:
                        with pool.If(most > r * BLOCK):
                            with pool.Fori(0, PAIRS) as i:
                                for j in range(2):
                                    scatter(over[l], l, j, r * PAIRS + i - PAIRS)
                                for j in range(2):
                                    pool.wait_ge(over[l].scattered[j], (r * PAIRS + i + (1 - PAIRS)) * 16)
                        with pool.Else():
                            pool.nop()
                        pool.nop()
                    pool.nop()
                with pool.Else():
                    pool.nop()
                for j in range(2):
                    pool.wait_ge(S.scattered[j], 16 * PAIRS)
                pool.sem_inc(rows_done, 1)

        @block.scalar
        def _(act):
            def load_gain(i):
                src = [norm_mix[0:1, :], norm_ffn[0:1, :], norm_mix[1:2, :], norm_ffn[1:2, :],
                       final_norm.rearrange("(a d) -> a d", a=1)][i]
                act.dma_start(gain[:], src.to_broadcast([P, D])).then_inc(gain_in, 16)

            def load_router(l):
                act.dma_start(wr[:, :, 0:NG], w_group[l].rearrange("(k p) n -> p k n", p=P)).then_inc(router_in[l], 16)
                act.dma_start(wr[:, :, NG:NR], w_expert[l].rearrange("(k p) n -> p k n", p=P)).then_inc(router_in[l], 16)
                act.dma_start(br[:, 0:NG], b_group[l:l + 1, :].to_broadcast([P, NG])).then_inc(router_in[l], 16)
                act.dma_start(br[:, NG:NR], b_expert[l:l + 1, :].to_broadcast([P, E])).then_inc(router_in[l], 16)

            def root(i, t):
                if i == 0:
                    act.wait_ge(x_in[t], 16)
                elif i % 2 == 1:
                    act.wait_ge(mix_used, TT * (i - 1) + 2 * t + 2)
                else:
                    act.wait_ge(h_ready, TT * (i // 2 - 1) + t + 1)
                nc.scalar.activation(squared, h[:, t, :], ACT.Square, accum_out=ss[:, t:t + 1]).then_inc(squares, 1)
                act.wait_ge(squares, TT * i + t + 1)
                if i > 0:
                    act.wait_ge(xr_ready, TT * (i - 1) + t + 1)
                nc.scalar.activation(rstd[:, t:t + 1], ss[:, t:t + 1], ACT.Sqrt,
                                     bias=eps[:], scale=1.0 / D).then_inc(root_ready, 1)

            def take_turned(i, t):
                if i in (0, 2):
                    if i == 2 and t == 0:
                        act.wait_ge(h_ready, 2)
                    for half in range(2):
                        act.wait_ge(xt_ps, 8 * i + 2 * t + half + 1)
                        nc.scalar.activation(parts(xt[:, 4 * half:4 * half + 4, t * P:(t + 1) * P]),
                                             ps[(2 * t + half) % 4][:].rearrange("p (a b) -> p a b", b=P), ACT.Copy)\
                            .then_inc(xt_high, 1)
                    return
                act.wait_ge(xt_ps, 8 * i + 2 * t + 1)
                nc.scalar.activation(xt[:, 0:4, t * P:(t + 1) * P],
                                     ps[2 * t % 4][:].rearrange("p (a b) -> p a b", b=P), ACT.Copy).then_inc(xt_even, 1)

            def norm(i):
                for t in range(TT):
                    root(i, t)
                    if t >= 1 and i < 4:
                        take_turned(i, t - 1)
                if i < 4:
                    take_turned(i, TT - 1)
                    act.wait_ge(xr_ready, TT * (i + 1))
                    load_gain(i + 1)

            for g in range(KV):
                for p in range(2):
                    s0 = g * HG + p * 4
                    act.dma_start(relT[s0:s0 + 4, :], rel_bias[:, g * HG + p:g * HG + HG:2].rearrange("b h -> h b"))\
                        .then_inc(rel_in, 16)
            load_gain(0)
            for g in range(KV):
                for p in range(2):
                    act.dma_start(sink[:, g, p * 4:p * 4 + 4],
                                  sinks[0:1, g * HG + p:g * HG + HG:2].to_broadcast([P, 4])).then_inc(attn_in, 16)
            act.dma_start(bq, b_qkv[0, 0:H * HD].rearrange("(j p) -> p j", p=P)).then_inc(attn_in, 16)
            act.dma_start(bk, b_qkv[0, H * HD:(H + KV) * HD].rearrange("(p a) -> p a", a=1)).then_inc(attn_in, 16)
            act.dma_start(bv, b_qkv[0, (H + KV) * HD:].rearrange("(p a) -> p a", a=1)).then_inc(attn_in, 16)
            act.dma_start(bo, b_o[0:1, :].to_broadcast([P, D])).then_inc(attn_in, 16)
            load_router(0)
            act.wait_ge(consts_ready, 7)
            def split_high(w, high):
                nc.scalar.activation(parts(high), w, ACT.Copy).then_inc(w_high, 1)

            norm(0)
            big_loaded(act, 0)
            for j in range(DT):
                if j >= 2:
                    act.wait_ge(qk_ps, j - 1)
                split_high(*query_weights(j))
            act.wait_ge(kv_in, 16)
            split_high(*key_value_weights())
            act.wait_ge(qk_ready, DT + 1)
            nc.scalar.activation(keys[HD:P, 0, :], keys[0:HD, 0, :], ACT.Copy)
            nc.scalar.activation(keys[0:HD, 1, :], keys[HD:P, 1, :], ACT.Copy).then_inc(keys_ready, 1)
            def att_exp(u):
                b = u % 3
                act.wait_ge(peak_ready, u + 1)
                lo = P if u < KV else 0
                nc.scalar.activation(sink_e[:, b, :], sink_e[:, b, :], ACT.Exp).then_inc(sink_ready, 1)
                for k in range(HG):
                    nc.scalar.activation(unit_scores[b][:, k, lo:], unit_scores[b][:, k, lo:], ACT.Exp,
                                         bias=peak[:, b, k:k + 1], accum_out=sums[:, b, k:k + 1])\
                        .then_inc(probs_ready, 1)

            def att_scale(u):
                b = u % 3
                lo = P if u < KV else 0
                act.wait_ge(rden_ready, 2 * u + 2)
                for k in range(HG // 2, HG):
                    nc.scalar.activation(unit_scores[b][:, k, lo:], unit_scores[b][:, k, lo:], ACT.Copy,
                                         scale=rden[:, b, k:k + 1]).then_inc(scaled_act, 1)

            def att_turn(u):
                for f in range(4):
                    act.wait_ge(pT_ps, 4 * u + f + 1)
                    nc.scalar.activation(probsT[:, 2 * f:2 * f + 2],
                                         turned_bank(u, f)[:].rearrange("p (a c q) -> p a c q", a=2, c=2),
                                         ACT.Copy).then_inc(pT_ready, 1)

            def att_take_out(u):
                n, g = u // KV, u % KV
                act.wait_ge(o_ps, u + 1)
                nc.scalar.activation(parts(xt[:, 4 * g:4 * g + 4, n * P:(n + 1) * P]),
                                     ps[6][:].rearrange("p (a b) -> p a b", b=P), ACT.Copy).then_inc(oT_high, 1)

            U = TT * KV
            att_exp(0)
            for u in range(U):
                if u + 1 < U:
                    att_exp(u + 1)
                att_scale(u)
                if u >= 1:
                    att_take_out(u - 1)
                att_turn(u)
            att_take_out(U - 1)

            def router(l):
                act.wait_ge(halves_ps, l + 1)
                nc.scalar.activation(logitsT[0:NR, :], ps[4][0:NR, :], ACT.Copy).then_inc(halves_ready, 1)
                act.wait_ge(shift_ready, 2 * l + 1)
                nc.scalar.activation(rt[:, :, 16:20], rt[:, :, 16:20], ACT.Exp).then_inc(exp_ready, 1)
                act.wait_ge(shift_ready, 2 * l + 2)
                nc.scalar.activation(rt[:, :, 20:21], rt[:, :, 20:21], ACT.Exp).then_inc(exp_ready, 1)

            def take(S, i):
                act.wait_ge(S.gathered, i + 1)
                for half in range(2):
                    ins = nc.scalar.activation(xg[:, 4 * half:4 * half + 4, :],
                                               ps[half][:].rearrange("p (a b) -> p a b", a=4), ACT.Copy)
                ins.then_inc(S.xg_ready, 1)

            def swish(S, n, j):
                act.wait_ge(S.gu_done, n + 1)
                nc.scalar.activation(silu[BLOCK:P, j, :], ps[2 + j][0:BLOCK, :], ACT.Silu).then_inc(S.silu_ready, 1)

            def take_hidden(S, n, j):
                act.wait_ge(S.turned, n + 1)
                nc.scalar.activation(hidT[:, j], ps[4 + j][:, 0:FT * BLOCK].rearrange("p (a b) -> p a b", a=FT),
                                     ACT.Copy).then_inc(S.hidT_ready, 1)

            def pair(S, i, last=False):
                for j in range(2):
                    swish(S, i * 2 + j, j)
                for j in range(2):
                    take_hidden(S, i * 2 + j, j)
                if not last:
                    take(S, i + 1)

            def experts(l):
                S = main[l]
                take(S, 0)
                with act.Fori(0, PAIRS - 1) as i:
                    pair(S, i)
                pair(S, PAIRS - 1, last=True)
                act.wait_ge(route_ready, l + 1)
                most = act.value_load(fullest[0:1, 0:1], min_val=0, max_val=T)
                with act.If(most > BLOCK):
                    with act.Fori(1, ROUNDS) as r:
                        with act.If(most > r * BLOCK):
                            with act.Fori(0, PAIRS) as i:
                                q = r * PAIRS + i - PAIRS
                                take(over[l], q)
                                pair(over[l], q, last=True)
                        with act.Else():
                            act.nop()
                        act.nop()
                    act.nop()
                with act.Else():
                    act.nop()

            norm(1)
            router(0)
            experts(0)
            def split_conv(j):
                if j * P % QC == 0:
                    q = j * P // QC
                    act.wait_ge(conv_in[q % 2], 16 * 3 * (q // 2 + 1))
                if j >= 2:
                    act.wait_ge(gates_ps, j - 1)
                else:
                    act.wait_ge(rows_done, 1)
                split_high(*conv_weights(j))

            def split_out(ks):
                for k in ks:
                    out_weights_wait(act, k)
                    split_high(*out_weights(k))

            split_conv(0)
            norm(2)
            for k in range(3):
                act.dma_start(cw[:, k, :], conv_w[0, k].rearrange("(j p) -> p j", p=P)).then_inc(router_in[1], 16)
            load_router(1)

            split_conv(1)
            for j in range(DT):
                act.wait_ge(gates_ps, j + 1)
                if j >= 2:
                    act.wait_ge(conv_ready, j - 1)
                nc.scalar.activation(c_gate[:, j % 2, :], ps[3 * (j % 2) + 1][:], ACT.Copy).then_inc(c_ready, 1)
                if j + 2 < DT:
                    split_conv(j + 2)
                if j == DT - 2:
                    act.wait_ge(w_out_in, 16)
                    split_out(range(5))
                if j == DT - 1:
                    split_out(range(5, DT))
            norm(3)
            router(1)
            experts(1)
            norm(4)

        @block.tensor
        def _(pe):
            def turn_tile(i, t):
                pe.wait_ge(xr_ready, TT * i + t + 1)
                for half in range(2):
                    f = 2 * t + half
                    if f >= 4:
                        pe.wait_ge(xt_odd if half else xt_even, TT * i + (f - 4) // 2 + 1)
                    for a in range(4):
                        d = half * 4 + a
                        mm = nc.tensor.transpose(ps[f % 4][:, a * P:(a + 1) * P],
                                                 xr[:, t, d * P:(d + 1) * P], ident[:])
                    mm.then_inc(xt_ps, 1)
                if t == TT - 1:
                    pe.wait_ge(xt_even, TT * (i + 1))
                    pe.wait_ge(xt_odd, TT * (i + 1))

            def turn(i):
                for t in range(TT):
                    turn_tile(i, t)

            def split_product(bank, left, left_low, right, right_low, start, stop):
                for a, b in ((left, right), (left, right_low), (left_low, right)):
                    mm = nc.tensor.matmul(bank, parts(a), parts(b), start=start and a is left and b is right,
                                          stop=stop and a is left_low)
                return mm

            pe.wait_ge(consts_ready, 7)
            turn(0)
            for j in range(DT):
                w, high = query_weights(j)
                pe.wait_ge(w_split, j + 1)
                if j >= 2:
                    pe.wait_ge(qk_ready, j - 1)
                for k in range(DT):
                    mm = split_product(ps[4 + j % 2][:], high[:, k, :], w[:, k, :], xt[:, k, :], xt_low[:, k],
                                       k == 0, k == DT - 1)
                mm.then_inc(qk_ps, 1)
            pe.wait_ge(bias_in, 16)
            for f in range(8):
                if f >= 2:
                    pe.wait_ge(bias_ready, f - 1)
                nc.tensor.matmul(ps[6 + f % 2][:], flip[:], bias_rev[:, f * 512:(f + 1) * 512],
                                 start=True, stop=True).then_inc(flip_ps, 1)
            w, high = key_value_weights()
            pe.wait_ge(w_split, KV_SPLIT + 1)
            for v in range(2):
                pe.wait_ge(qk_ready, DT - 1 + v)
                cols = slice(v * KV * HD, (v + 1) * KV * HD)
                for k in range(DT):
                    mm = split_product(ps[4 + v][:], high[:, k, cols], w[:, k, cols], xt[:, k, :], xt_low[:, k],
                                       k == 0, k == DT - 1)
                mm.then_inc(qk_ps, 1)
            pe.wait_ge(valuesT_ready, 1)
            for t in range(TT):
                mm = nc.tensor.transpose(ps[4][:, t * P:(t + 1) * P], valuesT[:, t * P:(t + 1) * P], ident[:])
            mm.then_inc(values_ps, 1)

            U = TT * KV

            def att_scores(u):
                n, g = u // KV, u % KV
                lo = 1 if n == 0 else 0
                for hh in range(HG):
                    if u >= 1 and hh % 4 == 0:
                        pe.wait_ge(score_ready, 8 * (u - 1) + hh + 4)
                    j, half = (g * HG + hh) // 2, hh % 2
                    slot = half * 4 + hh // 2
                    bank, col = slot // 2, (slot % 2) * 2 * P
                    r0 = half * HD
                    mm = nc.tensor.matmul(ps[bank][:, col + lo * P:col + 2 * P],
                                          queries(n)[r0:r0 + HD, j, :],
                                          keys[r0:r0 + HD, g, (n - 1 + lo) * P:(n + 1) * P],
                                          start=True, stop=True, skip_group_check=True)
                    if hh % 4 == 3:
                        mm.then_inc(score_ps, 1)

            def att_turn(u):
                n = u // KV
                for f in range(4):
                    if f < 2:
                        pe.wait_ge(scaled_dve, u + 1)
                    else:
                        pe.wait_ge(scaled_act, 4 * u + 2 * f - 2)
                    if 4 * u + f >= 3:
                        pe.wait_ge(pT_ready, 4 * u + f - 2)
                    for a in range(2):
                        for c in range(2):
                            if n == 0 and c == 0:
                                continue
                            mm = nc.tensor.transpose(turned_bank(u, f)[:, (2 * a + c) * P:(2 * a + c + 1) * P],
                                                     unit_scores[u % 3][:, 2 * f + a, c * P:(c + 1) * P], ident[:])
                    mm.then_inc(pT_ps, 1)

            def att_out(u):
                n, g = u // KV, u % KV
                if u >= 1:
                    pe.wait_ge(oT_ready, u)
                pe.wait_ge(pT_ready, 4 * u + 4)
                first = 1 if n == 0 else 0
                for c in range(first, 2):
                    for half in range(2):
                        mm = nc.tensor.matmul(ps[6][half * HD:(half + 1) * HD, :],
                                              values[:, n - 1 + c, g * HD:(g + 1) * HD],
                                              probsT[:, half * 4:half * 4 + 4, c, :],
                                              start=(c == first), stop=(c == 1))
                mm.then_inc(o_ps, 1)

            pe.wait_ge(qk_ready, DT + 2)
            pe.wait_ge(keys_ready, 1)
            att_scores(0)
            att_scores(1)
            for u in range(U):
                if u + 2 < U:
                    att_scores(u + 2)
                att_turn(u)
                att_out(u)

            def project(first, i, product):
                for t in range(TT):
                    for ks in ([range(5), range(5, DT)] if t == 0 else [range(DT)]):
                        for half in range(2):
                            f = 2 * t + half
                            if f >= 2:
                                pe.wait_ge(mix_used, first + f - 1)
                            for k in ks:
                                mm = product(ps[6 + f % 2][:], t, half, k)
                            if k == DT - 1:
                                mm.then_inc(mix_ps, 1)
                    if t >= 1:
                        turn_tile(i, t - 1)
                turn_tile(i, TT - 1)

            def attention_product(bank, t, half, k):
                if t == 0 and half == 0:
                    pe.wait_ge(wo_split, k + 1)
                w, high = mix_weights(k)
                cols = slice(half * HALF, (half + 1) * HALF)
                return split_product(bank, xt[:, k, t * P:(t + 1) * P], xt_low[:, k, t], high[:, cols], w[:, cols],
                                     k == 0, k == DT - 1)

            pe.wait_ge(oT_ready, U)
            project(0, 1, attention_product)

            def router(l):
                pe.wait_ge(router_in[l], 16 * (4 + (3 if l else 0)))
                for k in range(DT // 2):
                    for half in range(2):
                        d = half * DT // 2 + k
                        mm = nc.tensor.matmul(ps[4][half * BLOCK:half * BLOCK + NR, :], wr[:, d, :], xt[:, d, :],
                                              start=(k == 0), stop=(k == DT // 2 - 1))
                mm.then_inc(halves_ps, 1)
                pe.wait_ge(halves_ready, 2 * l + 2)
                for t in range(TT):
                    mm = nc.tensor.matmul(ps[7][:, t * NR:(t + 1) * NR], logitsT[:, t * P:(t + 1) * P], fold[:],
                                          start=True, stop=True)
                mm.then_inc(logits_ps, 1)
                pe.wait_ge(mask_ready, l + 1)
                nc.tensor.matmul(ps[5][:, 0:TT * E], upper[:], rt[:, :, 224:256], start=True, stop=False)
                pe.wait_ge(before_ready, l + 1)
                nc.tensor.matmul(ps[5][:, E:TT * E], ones[:], before[:, 0:TT - 1, :], start=False, stop=True)
                nc.tensor.matmul(ps[5][:, TT * E:(TT + 1) * E], ones[:], before[:, TT - 1, :],
                                 start=True, stop=True).then_inc(rank_ps, 1)

            def gather(S, i):
                pe.wait_ge(S.selected, i + 1)
                for d in range(DT):
                    for t in range(TT):
                        mm = nc.tensor.matmul(ps[d // 4][:, (d % 4) * P:(d % 4 + 1) * P], xr[:, t, d * P:(d + 1) * P],
                                              sel[:, t, :, :], start=(t == 0), stop=(t == TT - 1))
                for t in range(TT):
                    mm = nc.tensor.matmul(ps[4][:, 0:2], sel[:, t, :, :], dcol[:, t, :],
                                          start=(t == 0), stop=(t == TT - 1))
                mm.then_inc(S.gathered, 1)

            def gate_up(S, j, w, cuts=None):
                for k in range(DT):
                    if cuts and k % (DT // LAST_CUTS) == 0:
                        pe.wait_ge(cuts[k * LAST_CUTS // DT], 16)
                    for half in range(2):
                        mm = nc.tensor.matmul(ps[2 + j][half * BLOCK:(half + 1) * BLOCK, :],
                                              xg[:, k, j * BLOCK:(j + 1) * BLOCK], w[:, k, half * FF:(half + 1) * FF],
                                              start=(k == 0), stop=(k == DT - 1))
                mm.then_inc(S.gu_done, 1)

            def turn_hidden(S, n, j):
                pe.wait_ge(S.hid_ready, n + 1)
                pe.sem_inc(pe_mark, 1)
                for k in range(FT):
                    mm = nc.tensor.transpose(ps[4 + j][:, k * BLOCK:(k + 1) * BLOCK],
                                             hid[BLOCK:P, j, k * P:(k + 1) * P], ident[BLOCK:P, BLOCK:P])
                mm.then_inc(S.turned, 1)

            def down(S, n, j, w):
                pe.wait_ge(S.hidT_ready, n + 1)
                for k in range(FT):
                    for half in range(2):
                        mm = nc.tensor.matmul(ps[6 + j][half * BLOCK:(half + 1) * BLOCK, :], hidT[:, j, k, :],
                                              w[:, k, half * HALF:(half + 1) * HALF],
                                              start=(k == 0), stop=(k == FT - 1))
                mm.then_inc(S.down_done, 1)

            def experts(l):
                S = main[l]
                b0 = BIG_EXPERT[l]
                gather(S, 0)

                def up(i, j):
                    big_loaded(pe, b0 + j, i)
                    if j == 0:
                        pe.wait_ge(S.xg_ready, i + 1)
                    gate_up(S, j, big[:, big_slot(b0 + j)])

                def turn(m, odd, j):
                    turn_hidden(S, (m * 2 + odd) * 2 + j, j)

                def finish(m, odd, j):
                    down_loaded(pe, l, m, odd, j)
                    down(S, (m * 2 + odd) * 2 + j, j, down_slot(odd, j))

                def pair(m, odd):
                    i = m * 2 + odd
                    up(i, 0)
                    up(i, 1)
                    pe.wait_ge(S.where_ready, i + 1)
                    turn(m, odd, 0)
                    finish(m, odd, 0)
                    turn(m, odd, 1)
                    gather(S, i + 1)
                    finish(m, odd, 1)

                pair(0, 0)
                with pe.Fori(0, PAIRS // 2 - 1) as m:
                    pair(m, 1)
                    pair(m + 1, 0)
                up(PAIRS - 1, 0)
                gate_up(S, 1, big[:, big_slot(b0 + 1)], last_in[l])
                pe.wait_ge(S.where_ready, PAIRS)
                for j in range(2):
                    turn(PAIRS // 2 - 1, 1, j)
                    finish(PAIRS // 2 - 1, 1, j)
                pe.wait_ge(route_ready, l + 1)
                most = pe.value_load(fullest[0:1, 0:1], min_val=0, max_val=T)
                with pe.If(most > BLOCK):
                    with pe.Fori(1, ROUNDS) as r:
                        with pe.If(most > r * BLOCK):
                            with pe.Fori(0, PAIRS) as i:
                                q = r * PAIRS + i - PAIRS
                                gather(over[l], q)
                                pe.wait_ge(over[l].xg_ready, q + 1)
                                pe.wait_ge(over[l].where_ready, q + 1)
                                pe.wait_ge(over_in[l], (r * PAIRS + i + (1 - PAIRS)) * 64)
                                for j in range(2):
                                    gate_up(over[l], j, big[:, j])
                                for j in range(2):
                                    turn_hidden(over[l], q * 2 + j, j)
                                    down(over[l], q * 2 + j, j, small[:, j])
                        with pe.Else():
                            pe.nop()
                        pe.nop()
                    pe.nop()
                with pe.Else():
                    pe.nop()

            router(0)
            experts(0)
            turn(2)
            for j in range(DT):
                w, high = conv_weights(j)
                pe.wait_ge(w_split, CONV_SPLIT + j + 1)
                if j >= 2:
                    pe.wait_ge(conv_ready, j - 1)
                for g in range(3):
                    for k in range(DT):
                        mm = split_product(ps[3 * (j % 2) + g][:], high[:, 3 * k + g, :], w[:, 3 * k + g, :],
                                           xt[:, k, :], xt_low[:, k], k == 0, k == DT - 1)
                mm.then_inc(gates_ps, 1)

            def conv_product(bank, t, half, k):
                if t == 0 and half == 0:
                    pe.wait_ge(w_split, CONV_SPLIT + DT + k + 1)
                w, high = out_weights(k)
                cols = slice(half * HALF, (half + 1) * HALF)
                rows = slice(t * P, (t + 1) * P)
                return split_product(bank, gated[:, k, rows], gated_low[:, k, rows], high[:, cols], w[:, cols],
                                     k == 0, k == DT - 1)

            pe.wait_ge(conv_ready, DT)
            project(2 * TT, 3, conv_product)
            router(1)
            experts(1)

        @block.vector
        def _(dve):
            steps = [0]
            V = nc.vector

            def step(ins):
                ins.then_inc(dve_step, 1)
                steps[0] += 1
                dve.wait_ge(dve_step, steps[0])

            def norm_tile(i, t):
                dve.wait_ge(root_ready, TT * i + t + 1)
                step(V.reciprocal(rstd[:, t:t + 1], rstd[:, t:t + 1]))
                if t == 0:
                    dve.wait_ge(gain_in, 16 * (i + 1))
                V.scalar_tensor_tensor(out=xr[:, t, :], in0=h[:, t, :], scalar=rstd[:, t:t + 1],
                                       in1=gain[:], op0=ALU.mult, op1=ALU.mult).then_inc(xr_ready, 1)

            def take_turned(i, t):
                if i in (0, 2):
                    for half in range(2):
                        dve.wait_ge(xt_high, TT * i + 2 * t + half + 1)
                        ds = slice(4 * half, 4 * half + 4)
                        V.tensor_tensor(parts(xt_low[:, ds, t]), ps[(2 * t + half) % 4][:].rearrange(
                            "p (a b) -> p a b", b=P), parts(xt[:, ds, t * P:(t + 1) * P]), ALU.subtract)\
                            .then_inc(xt_odd if half else xt_even, 1)
                    return
                dve.wait_ge(xt_ps, 8 * i + 2 * t + 2)
                V.tensor_copy(xt[:, 4:8, t * P:(t + 1) * P],
                              ps[(2 * t + 1) % 4][:].rearrange("p (a b) -> p a b", b=P)).then_inc(xt_odd, 1)

            def norm(i, produce, ahead=False):
                if ahead:
                    produce(0)
                for t in range(TT):
                    if not ahead:
                        produce(t)
                    elif t + 1 < TT:
                        produce(t + 1)
                    norm_tile(i, t)
                    if t >= 1 and i < 4:
                        take_turned(i, t - 1)
                if i < 4:
                    take_turned(i, TT - 1)

            step(V.memset(toe[0:H, :], MASKED))
            dve.wait_ge(rel_in, 16 * 4)
            bounds = bucket_bounds()
            for k, (b, lo, hi) in enumerate(bounds):
                x0, x1 = 2 * P - 1 - hi, 2 * P - lo
                ins = V.tensor_copy(toe[0:H, x0:x1], relT[0:H, b:b + 1].to_broadcast([H, x1 - x0]))
            ins.then_inc(toe_ready, 1)
            norm(0, lambda t: dve.wait_ge(x_in[t], 16))
            step(V.tensor_tensor(fold[:], ident[:, 0:NR], ident[:, BLOCK:BLOCK + NR], ALU.add))
            dve.wait_ge(attn_in, 16 * 8)
            def split_low(n, w, high):
                dve.wait_ge(w_high, n + 1)
                V.tensor_tensor(parts(w), w, parts(high), ALU.subtract).then_inc(w_split, 1)

            split_low(0, *query_weights(0))
            split_low(1, *query_weights(1))
            for t in range(TT):
                ins = V.tensor_tensor(h[:, t, :], h[:, t, :], bo, ALU.add)
            step(ins)
            for j in range(DT):
                dve.wait_ge(qk_ps, j + 1)
                V.tensor_scalar(big[:, 0, 0:TT, j * P:(j + 1) * P], ps[4 + j % 2][:].rearrange("p (n c) -> p n c", c=P),
                                bq[:, j:j + 1], HD ** -0.5, ALU.add, ALU.mult).then_inc(qk_ready, 1)
                if j + 2 < DT:
                    split_low(j + 2, *query_weights(j + 2))
                elif j + 2 == DT:
                    split_low(KV_SPLIT, *key_value_weights())
            for f in range(8):
                dve.wait_ge(flip_ps, f + 1)
                V.tensor_copy(bias.rearrange("p a b c -> p (a b c)")[:, f * 512:(f + 1) * 512],
                              ps[6 + f % 2][:]).then_inc(bias_ready, 1)
            dve.wait_ge(qk_ps, DT + 1)
            for g in range(KV):
                half = slice(g * HD, (g + 1) * HD)
                ins = V.tensor_scalar(keys[half, g, :], ps[4][half, :], bk[half, :], None, ALU.add)
            ins.then_inc(qk_ready, 1)
            dve.wait_ge(qk_ps, DT + 2)
            V.tensor_scalar(valuesT, ps[5][:], bv, None, ALU.add).then_inc(valuesT_ready, 1)
            dve.wait_ge(values_ps, 1)
            V.tensor_copy(values, ps[4][:].rearrange("p (t n) -> p t n", t=TT)).then_inc(qk_ready, 1)
            dve.wait_ge(bias_ready, 8)

            U = TT * KV

            def att_bias(u):
                n, g, b = u // KV, u % KV, u % 3
                lo = P if n == 0 else 0
                if u >= 3:
                    dve.wait_ge(pT_ps, 4 * (u - 2))
                for hh in range(HG):
                    if hh % 4 == 0:
                        dve.wait_ge(score_ps, 2 * u + hh // 4 + 1)
                    k = (hh % 2) * 4 + hh // 2
                    ins = V.tensor_tensor_reduce(unit_scores[b][:, k, lo:], ps[k // 2][:, (k % 2) * 2 * P + lo:(k % 2 + 1) * 2 * P],
                                                 bias[:, g, k, lo:], 1.0, PAD, ALU.add, ALU.max, peak[:, b, k:k + 1])
                    ins.then_inc(score_ready, 1)
                dve.wait_ge(score_ready, HG * (u + 1))
                step(V.tensor_tensor(peak[:, b, :], peak[:, b, :], sink[:, g, :], ALU.max))
                step(V.tensor_scalar(peak[:, b, :], peak[:, b, :], -1.0, None, ALU.mult))
                V.tensor_tensor(sink_e[:, b, :], sink[:, g, :], peak[:, b, :], ALU.add).then_inc(peak_ready, 1)

            def att_scale(u):
                b = u % 3
                lo = P if u < KV else 0
                dve.wait_ge(sink_ready, u + 1)
                for half in range(2):
                    heads = slice(half * 4, half * 4 + 4)
                    dve.wait_ge(probs_ready, HG * u + half * 4 + 4)
                    step(V.tensor_tensor(rden[:, b, heads], sums[:, b, heads], sink_e[:, b, heads], ALU.add))
                    V.reciprocal(rden[:, b, heads], rden[:, b, heads]).then_inc(rden_ready, 1)
                    if half == 0:
                        dve.wait_ge(rden_ready, 2 * u + 1)
                        V.tensor_tensor(unit_scores[b][:, heads, lo:], unit_scores[b][:, heads, lo:],
                                        rden[:, b, heads].unsqueeze(2).to_broadcast([P, 4, 2 * P - lo]),
                                        ALU.mult).then_inc(scaled_dve, 1)

            def att_take_out(u):
                n, g = u // KV, u % KV
                dve.wait_ge(oT_high, u + 1)
                V.tensor_tensor(parts(xt_low[:, 4 * g:4 * g + 4, n]), ps[6][:].rearrange("p (a b) -> p a b", b=P),
                                parts(xt[:, 4 * g:4 * g + 4, n * P:(n + 1) * P]), ALU.subtract).then_inc(oT_ready, 1)

            att_bias(0)
            att_bias(1)
            for u in range(U):
                att_scale(u)
                if u + 2 < U:
                    att_bias(u + 2)
                if u >= 1:
                    att_take_out(u - 1)
            att_take_out(U - 1)

            def add_mix(l):
                def add(t):
                    for half in range(2):
                        f = 2 * t + half
                        dve.wait_ge(mix_ps, 2 * TT * l + f + 1)
                        hs = h[:, t, half * HALF:(half + 1) * HALF]
                        V.tensor_tensor(hs, ps[6 + f % 2][:], hs, ALU.add).then_inc(mix_used, 1)
                    dve.wait_ge(mix_used, 2 * TT * l + 2 * t + 2)
                return add

            def add_rows(l):
                def add(t):
                    dve.wait_ge(rows_in[t], 16 * (l + 1))
                    step(V.scalar_tensor_tensor(out=h[:, t, :], in0=stage[t][:, 0, :], scalar=gate1[:, t:t + 1],
                                                in1=h[:, t, :], op0=ALU.mult, op1=ALU.add))
                    V.scalar_tensor_tensor(out=h[:, t, :], in0=stage[t][:, 1, :], scalar=gate2[:, t:t + 1],
                                           in1=h[:, t, :], op0=ALU.mult, op1=ALU.add).then_inc(h_ready, 1)
                    dve.wait_ge(h_ready, TT * l + t + 1)
                return add

            def router(l):
                lg = rt[:, :, 32:32 + NR]
                gp, gm = rt[:, :, 0:8], rt[:, :, 8:16]
                eg = rt[:, :, 16:20]
                p2 = rt[:, :, 20:21]
                og = rt[:, :, 24:28]
                gi = rt[:, :, 28:29]
                i1, i2 = rt[:, :, 29:30], rt[:, :, 30:31]
                prod = rt[:, :, 72:104]
                ig, em = rt[:, :, 104:112], rt[:, :, 112:120]
                idx = rt[:, :, 120:128].bitcast(U32)
                gs, s2 = rt[:, :, 128:129], rt[:, :, 129:130]
                m2 = rt[:, :, 192:224]
                m12 = rt[:, :, 224:256]
                io = iota[:, 0:E].unsqueeze(1).to_broadcast([P, TT, E])
                V.memset(gp, PAD)
                dve.wait_ge(halves_ps, l + 1)
                V.tensor_copy(logitsT[BLOCK:BLOCK + NR, :], ps[4][BLOCK:BLOCK + NR, :]).then_inc(halves_ready, 1)
                dve.wait_ge(logits_ps, l + 1)
                step(V.tensor_tensor(lg, ps[7][:, 0:TT * NR].rearrange("p (t n) -> p t n", t=TT),
                                     br[:].unsqueeze(1).to_broadcast([P, TT, NR]), ALU.add))
                step(V.tensor_copy(gp[:, :, 0:NG], lg[:, :, 0:NG]))
                for t in range(TT):
                    ins = V.max(gm[:, t, :], gp[:, t, :])
                step(ins)
                for t in range(TT):
                    V.max_index(idx[:, t, :], gm[:, t, :], gp[:, t, :])
                V.tensor_tensor(eg, lg[:, :, 0:NG], gm[:, :, 0:1].to_broadcast([P, TT, NG]),
                                ALU.subtract).then_inc(shift_ready, 1)
                dve.wait_ge(shift_ready, 2 * l + 1)
                step(V.tensor_copy(gi, idx[:, :, 0:1]))
                step(V.tensor_tensor(og, iota[:, 0:NG].unsqueeze(1).to_broadcast([P, TT, NG]),
                                     gi.to_broadcast([P, TT, NG]), ALU.is_equal))
                for t in range(TT):
                    ins = V.tensor_tensor(prod[:, t, :].rearrange("p (g j) -> p g j", g=NG),
                                          lg[:, t, NG:NR].rearrange("p (g j) -> p g j", g=NG),
                                          og[:, t, :].unsqueeze(2).to_broadcast([P, NG, EG]), ALU.mult)
                step(ins)
                for t in range(TT):
                    ins = V.tensor_reduce(ig[:, t, :], prod[:, t, :].rearrange("p (g j) -> p j g", g=NG), X, ALU.add)
                step(ins)
                for t in range(TT):
                    ins = V.max(em[:, t, :], ig[:, t, :])
                step(ins)
                for t in range(TT):
                    V.max_index(idx[:, t, :], em[:, t, :], ig[:, t, :])
                V.tensor_tensor(p2, em[:, :, 1:2], em[:, :, 0:1], ALU.subtract).then_inc(shift_ready, 1)
                dve.wait_ge(shift_ready, 2 * l + 2)
                step(V.tensor_copy(rt[:, :, 29:31], idx[:, :, 0:2]))
                step(V.scalar_tensor_tensor(out=rt[:, :, 29:31], in0=gi.to_broadcast([P, TT, 2]), scalar=float(EG),
                                            in1=rt[:, :, 29:31], op0=ALU.mult, op1=ALU.add))
                V.tensor_tensor(m2, io, i2.to_broadcast([P, TT, E]), ALU.is_equal)
                step(V.tensor_tensor(m12, io, i1.to_broadcast([P, TT, E]), ALU.is_equal))
                step(V.tensor_tensor(m12, m12, m2, ALU.add))
                dve.sem_inc(mask_ready, 1)
                V.tensor_copy(before[:, 0, :], m12[:, 0, :])
                step(V.tensor_tensor(before[:, 1, :], m12[:, 0, :], m12[:, 1, :], ALU.add))
                step(V.tensor_tensor(before[:, 2, :], before[:, 1, :], m12[:, 2, :], ALU.add))
                step(V.tensor_tensor(before[:, 3, :], before[:, 2, :], m12[:, 3, :], ALU.add))
                dve.sem_inc(before_ready, 1)
                V.scalar_tensor_tensor(out=dest[:], in0=m2, scalar=-float(T),
                                       in1=base[:].unsqueeze(2).to_broadcast([P, TT, E]), op0=ALU.mult, op1=ALU.add)
                dve.wait_ge(exp_ready, 2 * l + 2)
                step(V.tensor_reduce(gs, eg, X, ALU.add))
                step(V.scalar_tensor_tensor(out=s2, in0=p2, scalar=1.0, in1=gs, op0=ALU.add, op1=ALU.mult))
                step(V.reciprocal(gate1[:].unsqueeze(2), s2))
                V.tensor_tensor(gate2[:].unsqueeze(2), gate1[:].unsqueeze(2), p2, ALU.mult)
                dve.wait_ge(rank_ps, l + 1)
                step(V.scalar_tensor_tensor(out=rank[:], in0=ps[5][:, 0:TT * E].rearrange("p (t e) -> p t e", t=TT),
                                            scalar=1.0, in1=m12, op0=ALU.add, op1=ALU.mult))
                step(V.tensor_scalar(rank[:], rank[:], -1.0, None, ALU.add))
                select(main[l], slice(0, 2))
                V.tensor_reduce(rt[:, 0, 130:131], ps[5][:, TT * E:(TT + 1) * E], X, ALU.max).then_inc(dve_step, 1)
                steps[0] += 1
                dve.wait_ge(dve_step, steps[0])
                V.tensor_copy(fullest[:], rt[:, 0, 130:131]).then_inc(route_ready, 1)

            def select(S, pair_at):
                ranks = rank[:, :, pair_at]
                V.tensor_tensor(sel, iota[:].unsqueeze(1).unsqueeze(1).to_broadcast([P, TT, 2, BLOCK]),
                                ranks.unsqueeze(3).to_broadcast([P, TT, 2, BLOCK]), ALU.is_equal)
                V.tensor_copy(dcol, dest[:, :, pair_at]).then_inc(S.selected, 1)

            def hidden(S, n, j):
                dve.wait_ge(S.silu_ready, n + 1)
                V.tensor_tensor(hid[BLOCK:P, j, :], silu[BLOCK:P, j, :], ps[2 + j][BLOCK:P, :], ALU.mult)\
                    .then_inc(S.hid_ready, 1)

            def find_rows(S, i, taken=None):
                dve.wait_ge(S.gathered, i + 1)
                if taken is not None:
                    dve.wait_ge(S.row_ready[0], taken)
                for j in range(2):
                    for c in range(2):
                        ins = V.tensor_scalar(where_f[c * BLOCK:(c + 1) * BLOCK, j:j + 1],
                                              ps[4][j * BLOCK:(j + 1) * BLOCK, j:j + 1], -2.0, float(2 * NONE + c),
                                              ALU.mult, ALU.add)
                ins.then_inc(S.where_ready, 1)

            def take_rows(S, n, i, j, free=None):
                dve.wait_ge(S.down_done, n + 1)
                if j == 0:
                    dve.wait_ge(S.where_ready, i + 1)
                    if free is not None:
                        for b in range(2):
                            dve.wait_ge(S.scattered[b], free)
                    V.tensor_copy(where, where_f)
                V.tensor_copy(y_rows[:, j, :], ps[6 + j][:]).then_inc(S.row_ready[j], 1)

            def experts(l):
                S = main[l]
                find_rows(S, 0)

                def pair(i, free, last=False):
                    if not last:
                        select(S, bass.ds(i * 2 + 2, 2))
                    hidden(S, i * 2, 0)
                    hidden(S, i * 2 + 1, 1)
                    take_rows(S, i * 2, i, 0, free)
                    if not last:
                        find_rows(S, i + 1, i + 1)
                    take_rows(S, i * 2 + 1, i, 1)

                pair(0, None)
                with dve.Fori(1, PAIRS - 1) as i:
                    pair(i, i * 16)
                pair(PAIRS - 1, (PAIRS - 1) * 16, last=True)
                dve.wait_ge(route_ready, l + 1)
                most = dve.value_load(fullest[0:1, 0:1], min_val=0, max_val=T)
                with dve.If(most > BLOCK):
                    for j in range(2):
                        dve.wait_ge(S.scattered[j], 16 * PAIRS)
                    with dve.Fori(1, ROUNDS) as r:
                        with dve.If(most > r * BLOCK):
                            V.tensor_scalar(rank[:], rank[:], -float(BLOCK), None, ALU.add).then_inc(round_ready[l], 1)
                            dve.wait_ge(round_ready[l], r)
                            dve.sem_inc(dve_mark, 1)
                            with dve.Fori(0, PAIRS) as i:
                                q = r * PAIRS + i - PAIRS
                                select(over[l], bass.ds(i * 2, 2))
                                find_rows(over[l], q)
                                hidden(over[l], q * 2, 0)
                                hidden(over[l], q * 2 + 1, 1)
                                take_rows(over[l], q * 2, q, 0)
                                take_rows(over[l], q * 2 + 1, q, 1)
                                for j in range(2):
                                    dve.wait_ge(over[l].scattered[j], (q + 1) * 16)
                        with dve.Else():
                            dve.nop()
                        dve.nop()
                    dve.nop()
                with dve.Else():
                    dve.nop()

            norm(1, add_mix(0))
            router(0)
            experts(0)

            split_low(CONV_SPLIT, *conv_weights(0))
            norm(2, add_rows(0), ahead=True)
            split_low(CONV_SPLIT + 1, *conv_weights(1))
            for b in range(2):
                ins = V.memset(z[:, b, 0:2], 0.0)
            step(ins)
            dve.wait_ge(router_in[1], 16 * 7)
            for j in range(DT):
                b = j % 2
                dve.wait_ge(gates_ps, j + 1)
                dve.wait_ge(c_ready, j + 1)
                step(V.tensor_tensor(z[:, b, 2:T + 2], c_gate[:, b, :], ps[3 * b + 2][:], ALU.mult))
                step(V.tensor_scalar(conv, z[:, b, 0:T], cw[:, 0, j:j + 1], None, ALU.mult))
                for k in (1, 2):
                    step(V.scalar_tensor_tensor(out=conv, in0=z[:, b, k:T + k], scalar=cw[:, k, j:j + 1],
                                                in1=conv, op0=ALU.mult, op1=ALU.add))
                step(V.tensor_tensor(conv, conv, ps[3 * b][:], ALU.mult))
                step(V.tensor_copy(parts(gated[:, j, :]), conv))
                V.tensor_tensor(parts(gated_low[:, j, :]), conv, parts(gated[:, j, :]), ALU.subtract).then_inc(conv_ready, 1)
                dve.wait_ge(conv_ready, j + 1)
                if j + 2 < DT:
                    split_low(CONV_SPLIT + j + 2, *conv_weights(j + 2))
                for k in (range(5) if j == DT - 2 else range(5, DT) if j == DT - 1 else []):
                    split_low(CONV_SPLIT + DT + k, *out_weights(k))
            norm(3, add_mix(1))
            router(1)
            experts(1)
            norm(4, add_rows(1), ahead=True)


_INS = ['x', 'norm_mix', 'norm_ffn', 'final_norm', 'rel_bias', 'attn_w_qkv', 'attn_b_qkv', 'attn_w_o',
        'attn_b_o', 'attn_sinks', 'conv_w_in', 'conv_w', 'conv_w_out', 'moe_w_group', 'moe_b_group',
        'moe_w_expert', 'moe_b_expert', 'moe_w_gate_up', 'moe_w_down']
_OUT = ((1, 512, 1024), 'float32')


def kernel(**inputs):
    import numpy as _np
    import concourse.bacc as _bacc
    from concourse import mybir as _mybir
    from concourse.bass_utils import run_bass_kernel_spmd as _run

    nc = _bacc.Bacc("TRN2", target_bir_lowering=False, num_devices=1)
    arrays, args = {}, []
    for name in _INS:
        a = _np.ascontiguousarray(inputs[name])
        arrays[f"in_{name}_dram"] = a
        args.append(nc.dram_tensor(f"in_{name}_dram", a.shape, _mybir.dt.from_np(a.dtype), kind="ExternalInput").ap())
    args.append(nc.dram_tensor("out_dram", _OUT[0], _mybir.dt.from_np(_np.dtype(_OUT[1])), kind="ExternalOutput").ap())
    build_trunk(nc, *args)
    r = _run(nc, [arrays], core_ids=[0])
    return r.results[0]["out_dram"]
```
